# Optimizing a Trainium2 kernel written in Bass

```python
import math
import jax, jax.numpy as jnp
from jax import lax
import numpy as np

D_MODEL = 1024
BATCH = 1
SEQ = 256
DEPTH = 2
DEC_BATCH = 1
DEC_SEQ = 256
PAST_LEN = 128

N_MIXERS = 2
N_A_LAYERS = (DEPTH + 1) // 2
N_B_LAYERS = DEPTH // 2
N_HEADS = 4
HEAD_DIM = D_MODEL // N_HEADS
CHUNK = 128
N_GATE_COLS = 4 * N_HEADS
M_INIT = -1e30
HEAD_NORM_EPS = 1e-6
CONV_W = 3
N_EXPERTS = 16
N_GROUPS = 4
EXPERTS_PER_GROUP = N_EXPERTS // N_GROUPS
TOP_K = 2
D_EXPERT = 256
LN_EPS = 1e-5
ALPHA = (2.0 * DEPTH) ** 0.25
BETA = (8.0 * DEPTH) ** -0.25

kernel_name = "hybrid_mlstm_shortconv_grouped_moe_encoder"

F32 = jnp.float32

def _layer_norm(x, g, b):
    xf = x.astype(F32)
    mu = jnp.mean(xf, axis=-1, keepdims=True)
    var = jnp.mean(jnp.square(xf - mu), axis=-1, keepdims=True)
    y = (xf - mu) * lax.rsqrt(var + LN_EPS) * g.astype(F32) + b.astype(F32)
    return y.astype(x.dtype)

def _mlstm_one_direction(q, k, v, log_i, log_f):
    bsz, nh, seq, dh = q.shape
    nc = seq // CHUNK

    def chunks(a):
        a = a.reshape((bsz, nh, nc, CHUNK) + a.shape[3:])
        return jnp.moveaxis(a, 2, 0)

    tril = jnp.tril(jnp.ones((CHUNK, CHUNK), dtype=bool))

    def step(carry, xs):
        c_prev, n_prev, m_prev = carry
        qb, kb, vb, ib, fb = xs
        f_cum = jnp.cumsum(fb, axis=-1)
        d_log = f_cum[..., :, None] - f_cum[..., None, :] + ib[..., None, :]
        d_log = jnp.where(tril, d_log, -jnp.inf)
        inter = f_cum + m_prev[..., None]
        m_row = jnp.maximum(jnp.max(d_log, axis=-1), inter)
        w = jnp.exp(d_log - m_row[..., None])
        s = jnp.einsum("bhid,bhjd->bhij", qb, kb) * w
        a_inter = jnp.exp(inter - m_row)
        num = jnp.einsum("bhij,bhjd->bhid", s, vb) + a_inter[..., None] * jnp.einsum("bhid,bhde->bhie", qb, c_prev)
        den = jnp.sum(s, axis=-1) + a_inter * jnp.einsum("bhid,bhd->bhi", qb, n_prev)
        h = num / jnp.maximum(jnp.abs(den), jnp.exp(-m_row))[..., None]
        f_tot = f_cum[..., -1]
        g = f_tot[..., None] - f_cum + ib
        m_new = jnp.maximum(f_tot + m_prev, jnp.max(g, axis=-1))
        wk = jnp.exp(g - m_new[..., None])
        decay = jnp.exp(f_tot + m_prev - m_new)
        c_new = decay[..., None, None] * c_prev + jnp.einsum("bhjd,bhje->bhde", kb * wk[..., None], vb)
        n_new = decay[..., None] * n_prev + jnp.einsum("bhj,bhjd->bhd", wk, kb)
        return (c_new, n_new, m_new), h

    init = (jnp.zeros((bsz, nh, dh, dh), F32), jnp.zeros((bsz, nh, dh), F32), jnp.full((bsz, nh), M_INIT, F32))
    _, h = lax.scan(step, init, (chunks(q), chunks(k), chunks(v), chunks(log_i), chunks(log_f)))
    return jnp.moveaxis(h, 0, 2).reshape(bsz, nh, seq, dh)

def _mlstm_mixer(x, w_in, b_gate, norm_g, w_out):
    bsz, seq, _ = x.shape
    proj = x @ w_in
    q, k, v, o = (proj[..., j * D_MODEL:(j + 1) * D_MODEL] for j in range(4))
    gates = proj[..., 4 * D_MODEL:].astype(F32) + b_gate.astype(F32)
    gates = gates.reshape(bsz, seq, 4, N_HEADS).transpose(2, 0, 3, 1)
    i_fw, f_fw, i_bw, f_bw = gates[0], gates[1], gates[2], gates[3]

    def heads(a):
        return a.reshape(bsz, seq, N_HEADS, HEAD_DIM).transpose(0, 2, 1, 3).astype(F32)

    qh = heads(q)
    kh = heads(k) * (HEAD_DIM ** -0.5)
    vh = heads(v)
    h_fw = _mlstm_one_direction(qh, kh, vh, i_fw, jax.nn.log_sigmoid(f_fw))
    flip = lambda a: jnp.flip(a, axis=2)
    h_bw = flip(_mlstm_one_direction(flip(qh), flip(kh), flip(vh), flip(i_bw), flip(jax.nn.log_sigmoid(f_bw))))
    h = h_fw + h_bw
    mu = jnp.mean(h, axis=-1, keepdims=True)
    var = jnp.mean(jnp.square(h - mu), axis=-1, keepdims=True)
    hn = (h - mu) * lax.rsqrt(var + HEAD_NORM_EPS)
    hn = hn.transpose(0, 2, 1, 3).reshape(bsz, seq, D_MODEL) * norm_g.astype(F32)
    y = (jax.nn.sigmoid(o.astype(F32)) * hn).astype(x.dtype)
    return y @ w_out

def _shortconv_mixer(x, w_in, conv_w, w_out):
    proj = x @ w_in
    b_gate = proj[..., :D_MODEL]
    c_gate = proj[..., D_MODEL:2 * D_MODEL]
    hv = proj[..., 2 * D_MODEL:]
    u = c_gate * hv
    kern = conv_w.astype(u.dtype)[:, None, :]
    conv = lax.conv_general_dilated(u, kern, window_strides=(1,), padding="SAME",
                                    dimension_numbers=("NWC", "WIO", "NWC"),
                                    feature_group_count=D_MODEL)
    return (b_gate * conv) @ w_out

def _grouped_moe(x, router_w, router_b, w_gu, w_down):
    bsz, seq, dm = x.shape
    t = x.reshape(-1, dm)
    logits = (t @ router_w).astype(F32) + router_b.astype(F32)
    probs = jax.nn.softmax(logits, axis=-1)
    grouped = probs.reshape(-1, N_GROUPS, EXPERTS_PER_GROUP)
    group_score = jnp.sum(lax.top_k(grouped, TOP_K)[0], axis=-1)
    g_sel = jnp.argmax(group_score, axis=-1)
    in_group = (jnp.arange(N_EXPERTS) // EXPERTS_PER_GROUP)[None, :] == g_sel[:, None]
    top_v, top_i = lax.top_k(jnp.where(in_group, probs, -1.0), TOP_K)
    gates = top_v / jnp.sum(top_v, axis=-1, keepdims=True)
    combine = jnp.sum(jax.nn.one_hot(top_i, N_EXPERTS, dtype=F32) * gates[..., None], axis=1)
    out = jnp.zeros(t.shape, F32)
    for e in range(N_EXPERTS):
        gu = t @ w_gu[e]
        h = jax.nn.silu(gu[:, :D_EXPERT]) * gu[:, D_EXPERT:]
        out = out + combine[:, e:e + 1] * (h @ w_down[e]).astype(F32)
    return out.astype(x.dtype).reshape(bsz, seq, dm)

def _trunk(x, router_w, router_b, mlstm_w_in, mlstm_b_gate, mlstm_norm_g, mlstm_w_out,
           conv_w_in, conv_w, conv_w_out, ln1_g, ln1_b, moe_w_gu, moe_w_down, ln2_g, ln2_b):
    for i in range(DEPTH):
        j = i // N_MIXERS
        if i % N_MIXERS == 0:
            mix = _mlstm_mixer(x, mlstm_w_in[j], mlstm_b_gate[j], mlstm_norm_g[j], mlstm_w_out[j])
        else:
            mix = _shortconv_mixer(x, conv_w_in[j], conv_w[j], conv_w_out[j])
        x = _layer_norm(ALPHA * x + mix, ln1_g[i], ln1_b[i])
        ffn = _grouped_moe(x, router_w, router_b, moe_w_gu[i], moe_w_down[i])
        x = _layer_norm(ALPHA * x + ffn, ln2_g[i], ln2_b[i])
    return x

def _normal(k, shape, scale):
    return jax.random.normal(k, shape, F32) * scale

def setup_inputs(seed: int = 0) -> dict:
    key = jax.random.key(seed)
    ks = jax.random.split(key, 20)
    d = D_MODEL
    i_bias = _normal(ks[5], (N_A_LAYERS, 2, N_HEADS), 0.1)
    f_bias = jnp.linspace(3.0, 6.0, N_HEADS, dtype=F32)[None, None, :] + _normal(ks[6], (N_A_LAYERS, 2, N_HEADS), 0.1)
    b_gate = jnp.stack([i_bias, f_bias], axis=2).reshape(N_A_LAYERS, N_GATE_COLS)
    return {
        "x_prompt": _normal(ks[0], (BATCH, SEQ, d), 1.0),
        "x_sample": _normal(ks[1], (DEC_BATCH, DEC_SEQ, d), 1.0),
        "router_w": _normal(ks[2], (d, N_EXPERTS), d ** -0.5),
        "router_b": _normal(ks[3], (N_EXPERTS,), 0.01),
        "mlstm_w_in": _normal(ks[4], (N_A_LAYERS, d, 4 * d + N_GATE_COLS), d ** -0.5),
        "mlstm_b_gate": b_gate,
        "mlstm_norm_g": 1.0 + _normal(ks[7], (N_A_LAYERS, d), 0.02),
        "mlstm_w_out": _normal(ks[8], (N_A_LAYERS, d, d), BETA * d ** -0.5),
        "conv_w_in": _normal(ks[9], (N_B_LAYERS, d, 3 * d), d ** -0.5),
        "conv_w": _normal(ks[10], (N_B_LAYERS, CONV_W, d), CONV_W ** -0.5),
        "conv_w_out": _normal(ks[11], (N_B_LAYERS, d, d), BETA * d ** -0.5),
        "ln1_g": 1.0 + _normal(ks[12], (DEPTH, d), 0.02),
        "ln1_b": _normal(ks[13], (DEPTH, d), 0.02),
        "moe_w_gu": _normal(ks[14], (DEPTH, N_EXPERTS, d, 2 * D_EXPERT), d ** -0.5),
        "moe_w_down": _normal(ks[15], (DEPTH, N_EXPERTS, D_EXPERT, d), BETA * D_EXPERT ** -0.5),
        "ln2_g": 1.0 + _normal(ks[16], (DEPTH, d), 0.02),
        "ln2_b": _normal(ks[17], (DEPTH, d), 0.02),
    }

def reference(x_prompt, x_sample, router_w, router_b, mlstm_w_in, mlstm_b_gate, mlstm_norm_g, mlstm_w_out,
              conv_w_in, conv_w, conv_w_out, ln1_g, ln1_b, moe_w_gu, moe_w_down, ln2_g, ln2_b):
    y_prompt = _trunk(x_prompt, router_w, router_b, mlstm_w_in, mlstm_b_gate, mlstm_norm_g, mlstm_w_out,
                      conv_w_in, conv_w, conv_w_out, ln1_g, ln1_b, moe_w_gu, moe_w_down, ln2_g, ln2_b)
    y_sample = _trunk(x_sample, router_w, router_b, mlstm_w_in, mlstm_b_gate, mlstm_norm_g, mlstm_w_out,
                      conv_w_in, conv_w, conv_w_out, ln1_g, ln1_b, moe_w_gu, moe_w_down, ln2_g, ln2_b)
    return (y_prompt, y_sample)


_drawn_inputs = setup_inputs


def setup_inputs(seed=0):
    import zlib

    import numpy as np

    out = dict(_drawn_inputs(seed))
    spreads = {}
    factors = {}
    for name, (base, spread) in spreads.items():
        noise = np.random.default_rng([zlib.crc32(name.encode()), seed]).standard_normal(out[name].shape)
        drawn = base * np.exp(spread * noise) if base else spread * noise
        out[name] = __import__('jax').numpy.asarray(drawn.astype(out[name].dtype))
    for name, factor in factors.items():
        out[name] = (out[name] * factor).astype(out[name].dtype)
    return out
```

```python
from contextlib import ExitStack

import concourse.bass as bass
from concourse import mybir

ALU = mybir.AluOpType
ACT = mybir.ActivationFunctionType
AX = mybir.AxisListType
F32 = mybir.dt.float32
F32R = mybir.dt.float32r
I32 = mybir.dt.int32
U32 = mybir.dt.uint32

P = 128
NO_ROW = 2048.0
NEG = -1e30


class Steps:

    def __init__(self, engine, sem):
        self.engine, self.sem, self.n, self.turn = engine, sem, 0, 0

    def __call__(self, instruction):
        instruction.then_inc(self.sem, 1)
        self.n += 1

    def wait(self):
        self.engine.wait_ge(self.sem, self.turn + self.n)

    def loop(self, turn, per_turn):
        self.turn, self.before, self.per_turn = turn * per_turn, self.n, per_turn

    def end(self, turns):
        assert self.n - self.before == self.per_turn, (self.n - self.before, self.per_turn)
        self.turn, self.n = 0, self.before + turns * self.per_turn


def trunk(nc, x_prompt, x_sample, router_w, router_b, mlstm_w_in, mlstm_b_gate, mlstm_norm_g, mlstm_w_out,
          conv_w_in, conv_w, conv_w_out, ln1_g, ln1_b, moe_w_gu, moe_w_down, ln2_g, ln2_b,
          y_prompt, y_sample, PLACES=P):
    S = x_prompt.shape[1]
    D = x_prompt.shape[2]
    T = 2 * S
    NT = T // P
    KC = D // P
    E = moe_w_gu.shape[1]
    NG, GE = 4, E // 4
    FE = moe_w_down.shape[2]
    NH = mlstm_b_gate.shape[1] // 4
    HD = D // NH
    VW = HD + 2
    ALPHA = float((2.0 * 2) ** 0.25)
    LN_EPS, HEAD_EPS = 1e-5, 1e-6
    ROUNDS = -(-T // PLACES)
    UNIT = 2048
    CG = 512
    assert (S, D, NT, KC, NH, HD, FE) == (256, 1024, 4, 8, 4, 256, 256)

    MIX1_UNITS, MIX2_UNITS, MOE_UNITS = 20, 16, 3 * E
    SPLIT0 = [MIX1_UNITS, MIX1_UNITS + 2 * E + MIX2_UNITS]
    SPLIT_CONV = MIX1_UNITS + 2 * E
    HL_CREDIT = 2
    BANK_CREDIT = 8
    RING1, RINGM, RING2 = 4, 12, 6
    phases = [(RING1, MIX1_UNITS), (RINGM, MOE_UNITS), (RING2, MIX2_UNITS), (RINGM, MOE_UNITS)]
    before = []
    tally = [0] * RINGM
    for ring, units in phases:
        before.append(list(tally))
        for u in range(units):
            tally[u % ring] += 1

    ctx = ExitStack()
    with ctx:
        def sb(name, shape, dt=F32):
            return ctx.enter_context(nc.sbuf_tensor(name, shape, dt))

        def sem(name):
            return ctx.enter_context(nc.semaphore(name))

        arena = sb("arena", [P, 28704])
        xt_hi = sb("xt_hi", [P, KC, T], F32R)
        xt_lo = sb("xt_lo", [P, KC, T], F32R)
        w_hi = sb("w_hi", [P, 2, UNIT], F32R)
        w_lo = sb("w_lo", [P, 2, UNIT], F32R)
        ln_g = sb("ln_g", [P, D])
        ln_b = sb("ln_b", [P, D])
        temp = sb("temp", [P, 3072])
        ident = sb("ident", [P, P])
        pick_head = sb("pick_head", [NH, NH, P])
        mask_fw, mask_bw = ln_b[:, 0:S], ln_b[:, S:2 * S]
        earlier = sb("earlier", [P, P])
        all_ones = sb("all_ones", [P, P])
        place_no = sb("place_no", [P, P])
        gate_w_hi = sb("gate_w_hi", [P, KC, 16], F32R)
        gate_w_lo = sb("gate_w_lo", [P, KC, 16], F32R)
        rout_w_hi = sb("rout_w_hi", [P, KC, E], F32R)
        rout_w_lo = sb("rout_w_lo", [P, KC, E], F32R)
        gate_b = sb("gate_b", [16, 1])
        rout_b = sb("rout_b", [E, 1])
        eps_ln = sb("eps_ln", [P, 1])
        eps_head = sb("eps_head", [P, 1])
        taps = sb("taps", [P, 3, KC])
        cols = sb("cols", [P, 2, 2, NT, NH])
        exp_neg_m = sb("exp_neg_m", [P, 2, NT, NH])
        den = sb("den", [P, 4])
        den_neg = sb("den_neg", [P, 4])
        den_rec = sb("den_rec", [P, 8, 4])
        stats = sb("stats", [P, NT, 2, 6])
        mean_var = sb("mean_var", [P, NT, 2])
        std = sb("std", [P, NT])
        rstd = sb("rstd", [P, NT])
        head_stats = sb("head_stats", [P, 8, 2, 6])
        head_mv = sb("head_mv", [P, 8, 2, 2])
        head_std = sb("head_std", [P, 8, 2])
        head_rstd = sb("head_rstd", [P, 8, 2])
        token_no = sb("token_no", [P, NT])
        group_first = sb("group_first", [P, NG])
        expert_first = sb("expert_first", [P, E])
        r_one = sb("r_one", [P, NT])
        r_sum = sb("r_sum", [P, NT])
        r_v1 = sb("r_v1", [P, NT])
        r_v2 = sb("r_v2", [P, NT])
        is_top1 = sb("is_top1", [P, NT, E])
        is_top2 = sb("is_top2", [P, NT, E])
        chosen_pad = sb("chosen_pad", [P, 2 * NT + 1, E])
        chosen = chosen_pad[:, NT:2 * NT, :]
        place = sb("place", [P, NT, E])
        values = sb("values", [P, NT, E, 2], F32R)
        gate_of = sb("gate_of", [P, NT, 2])
        r_max = sb("r_max", [P, 1])
        most = sb("most", [P, 1], I32)
        rows_of = sb("rows_of", [P, E, 2], U32)

        ps = ctx.enter_context(nc.psum_tensor("ps", [P, 8, 512], F32))

        x_dram = [nc.dram_tensor(f"x_after_{n}", (T, D), F32, kind="Internal").ap() for n in range(3)]
        y_dram = [nc.dram_tensor(f"expert_out_{n}", (2 * T, D), F32, kind="Internal").ap() for n in range(2)]

        def raw(slot):
            return arena[:, slot * UNIT:(slot + 1) * UNIT]

        def words(at, n):
            return arena[:, at:at + n]

        qT = words(8192, 4096).rearrange("p (c t) -> p c t", c=KC)
        kT = words(12288, 4096).rearrange("p (c t) -> p c t", c=KC)
        v_ext = words(16384, NT * NH * VW).rearrange("p (t h d) -> p t h d", t=NT, h=NH)
        o_sig = words(20512, 4096).rearrange("p (t d) -> p t d", t=NT)
        x_in = qT.rearrange("p c t -> p (c t)").rearrange("p (t d) -> p t d", t=NT)
        rest = 24608
        z = words(rest, 4096).rearrange("p (t d) -> p t d", t=NT)
        rows_i = arena[0:NH, rest:rest + 1024].rearrange("p (r t) -> p r t", r=2)
        rows_f = arena[0:NH, rest + 1024:rest + 2048].rearrange("p (r t) -> p r t", r=2)
        rows_l = arena[0:NH, rest + 2048:rest + 3072].rearrange("p (r t) -> p r t", r=2)
        rows_a = arena[0:NH, rest + 3072:rest + 4096].rearrange("p (r t) -> p r t", r=2)
        rows_c = temp[0:NH, 0:1024].rearrange("p (r t) -> p r t", r=2)
        rows_m = temp[0:NH, 1024:2048].rearrange("p (r t) -> p r t", r=2)
        exps = temp[:, 0:1536].rearrange("p (b n) -> p b n", b=2)
        probs = temp[:, 1536:3072].rearrange("p (b n) -> p b n", b=2)
        gates_T = temp[0:16, 2048:2048 + T]
        xg = words(rest, 2048).rearrange("p (b d) -> p b d", b=2)
        ye = words(rest + 2048, 2048).rearrange("p (b d) -> p b d", b=2)
        one_hot = xt_hi[:, :, 2 * P:3 * P].rearrange("p (b t) s -> p b t s", b=2)
        logits_T = temp[0:E, 0:T]
        silu_g = temp[:, 1024:1536].rearrange("p (b f) -> p b f", b=2)
        h_tok = temp[:, 1536:2048].rearrange("p (b f) -> p b f", b=2)
        h_T = temp[:, 2048:2560].rearrange("p (b k s) -> p b k s", b=2, k=2)
        gate_w = temp[:, 2560:2688].rearrange("p (k n) -> p k n", k=KC)
        rout_w = temp[:, 2688:2816].rearrange("p (k n) -> p k n", k=KC)
        r_log, r_prob, r_a, r_b = (temp[:, 2560 + 64 * n:2624 + 64 * n].rearrange("p (t e) -> p t e", t=NT)
                                   for n in range(4))
        r_pair = temp[:, 2816:2912].rearrange("p (g n) -> p g n", g=NT * NG)
        r_score, r_group = (temp[:, at:at + 16].rearrange("p (t g) -> p t g", t=NT) for at in (2912, 2928))
        conv_rows = temp[0:3 * KC, 2560:2688]
        y_back = words(6 * UNIT, 4096).rearrange("p (b k d) -> p b k d", b=2, k=2)
        c_T = words(6 * UNIT, 2048).rearrange("p (c t) -> p c t", c=4)
        u_T = words(7 * UNIT, 2048).rearrange("p (c t) -> p c t", c=4)
        conv_T = words(8 * UNIT, 2048).rearrange("p (c t) -> p c t", c=4)
        g_T = words(9 * UNIT, 4096).rearrange("p (c t) -> p c t", c=KC)
        late_xT = words(3 * UNIT, 1024).rearrange("p (c s) -> p c s", c=KC)

        s_x = [sem(f"x_loaded{t}") for t in range(NT)]
        s_par = sem("small_weights_loaded")
        s_cwl = sem("taps_loaded")
        s_raw = [sem(f"raw_loaded{s}") for s in range(RINGM)]
        s_const = sem("constants_made")
        s_hi = sem("unit_hi_ready")
        s_lo = sem("unit_lo_ready")
        s_hl = sem("unit_multiplied")
        s_bank = sem("bank_summed")
        s_free = sem("bank_evacuated")
        s_tr = sem("tile_half_transposed")
        s_xth = sem("xt_hi_ready")
        s_xtl = sem("xt_lo_ready")
        s_small = sem("small_split")
        s_gmm = sem("gates_multiplied")
        s_gb = sem("gates_biased")
        s_grow = sem("gates_transposed")
        s_rows = sem("gate_rows_read")
        s_soft = sem("softplus_steps")
        s_rowsd = sem("gate_rows_done")
        s_colmm = sem("columns_transposed")
        s_cols = sem("columns_read")
        s_em = sem("exp_neg_m_ready")
        s_mb = sem("maxima_spread")
        s_st = sem("scores_ready")
        s_e = sem("exponents_ready")
        s_exp = sem("exps_ready")
        s_p = sem("weights_ready")
        s_av = sem("heads_multiplied")
        s_rec = sem("denominators_ready")
        s_fwd = sem("forward_scaled")
        s_hh = sem("heads_ready")
        s_hstd = sem("head_std_ready")
        s_og = sem("o_times_norm_ready")
        s_y = sem("mixer1_tile_ready")
        s_lnp = sem("norm_weights_loaded")
        s_res = [sem(f"residual_loaded{t}") for t in range(NT)]
        s_stat = sem("norm_stats_ready")
        s_std = sem("norm_std_ready")
        s_zn = sem("normalised_ready")
        s_xr = sem("x_tile_ready")
        s_st_x = [sem(f"x_stored{t}") for t in range(NT)]
        s_yb = [sem(f"results_loaded{b}") for b in range(2)]
        s_ax = sem("residual_scaled")
        s_sum2 = sem("results_summed")
        s_lg = sem("logits_multiplied")
        s_lb = sem("logits_biased")
        s_lt = sem("logits_transposed")
        s_rlog = sem("logits_shifted")
        s_rexp = sem("router_exps_ready")
        s_chosen = sem("experts_chosen")
        s_rank = sem("places_multiplied")
        s_routed = sem("routing_ready")
        s_xg0 = sem("gather_buffers_cleared")
        s_oh = sem("one_hot_ready")
        s_ixm = sem("rows_multiplied")
        s_ix = sem("row_numbers_ready")
        s_gat = [sem(f"gathered{b}") for b in range(2)]
        s_gtr = sem("gathered_transposed")
        s_ghi = sem("gathered_hi_ready")
        s_glo = sem("gathered_lo_ready")
        s_silu = sem("silu_ready")
        s_h = sem("hidden_ready")
        s_htr = sem("hidden_transposed")
        s_ht = sem("hidden_transposed_read")
        s_dn = sem("down_multiplied")
        s_ye = sem("expert_result_read")
        s_sca = [sem(f"scattered{b}") for b in range(2)]
        s_cev = sem("c_read")
        s_hev = sem("h_or_b_read")
        s_conv = sem("convolved_ready")
        s_cwt = sem("taps_transposed")
        s_taps = sem("taps_ready")
        s_ghx = sem("g_hi_ready")
        s_glx = sem("g_lo_ready")
        s_dve = sem("vector_steps")
        s_pool = sem("gpsimd_steps")
        s_act = sem("scalar_steps")
        late = [{k: sem(f"late{n}_{k}") for k in (
            "w", "free", "oh", "ixm", "ix", "gat", "tr", "xt", "gu", "silu", "h", "htr", "ht", "dn", "ye", "sca")}
            for n in range(2)]

        def raw_count(phase, u, turn=0):
            ring = phases[phase][0]
            return (turn + (before[phase][u % ring] + u // ring + 1)) * 16

        def wait_bank(eng, group, unit, c):
            if c < 3:
                eng.wait_ge(s_bank, group * 3 + (c + 1))
            else:
                eng.wait_ge(s_hl, unit + (HL_CREDIT + 1))

        block = ctx.enter_context(nc.Block())

        @block.sync
        def _(sp):
            x_tiles = [x_prompt[0, 0:P, :], x_prompt[0, P:S, :], x_sample[0, 0:P, :], x_sample[0, P:S, :]]

            def rows4(w, k0, c0):
                return w[k0 * P:(k0 + 4) * P, c0:c0 + CG].rearrange("(k p) n -> p k n", p=P)

            def load(slot, src, k):
                sp.dma_start(raw(slot).rearrange("p (k n) -> p k n", k=k), src).then_inc(s_raw[slot], 16)

            w_in, w_out, cw_in, cw_out = mlstm_w_in[0], mlstm_w_out[0], conv_w_in[0], conv_w_out[0]
            for t in range(NT):
                sp.dma_start(x_in[:, t, :], x_tiles[t]).then_inc(s_x[t], 16)
                if t == 0:
                    sp.dma_start(gate_w[:, :, :], w_in[:, 4 * D:4 * D + 16].rearrange("(k p) n -> p k n", p=P)
                                 ).then_inc(s_par, 16)
                    sp.dma_start(gate_b[:, :], mlstm_b_gate.rearrange("o n -> n o")).then_inc(s_par, 16)
            u = 0
            for half in range(2):
                for part in range(4):
                    for kh in range(2):
                        if u >= RING1:
                            sp.wait_ge(s_lo, u - RING1 + 1)
                        load(u % RING1, rows4(w_in, 4 * kh, part * D + half * CG), 4)
                        if u == 3:
                            sp.dma_start(rout_w[:, :, :], router_w.rearrange("(k p) n -> p k n", p=P)
                                         ).then_inc(s_par, 16)
                            sp.dma_start(rout_b[:, :], router_b.rearrange("(n o) -> n o", o=1)
                                         ).then_inc(s_par, 16)
                        u += 1
            for half in range(2):
                for kh in range(2):
                    sp.wait_ge(s_lo, u - RING1 + 1)
                    load(u % RING1, rows4(w_out, 4 * kh, half * CG), 4)
                    u += 1

            def expert_loads(layer, turn, first):
                phase = 1 + 2 * layer
                split_phase = SPLIT0[layer]
                for j in range(4):
                    e = turn * 4 + j
                    for k in range(3):
                        u = 3 * j + k
                        if first and layer == 0:
                            if u < RING1:
                                sp.wait_ge(s_lo, MIX1_UNITS - RING1 + 1 + u)
                            else:
                                sp.wait_ge(s_tr, 16)
                        elif first:
                            if u < RING2:
                                last = max(v for v in range(MIX2_UNITS) if v % RING2 == u)
                                sp.wait_ge(s_lo, SPLIT_CONV + last + 1)
                            else:
                                sp.wait_ge(s_glx, KC)
                        elif k < 2:
                            sp.wait_ge(s_lo, turn * 8 + (split_phase - 8 + 2 * j + k + 1))
                        else:
                            sp.wait_ge(s_dn, turn * 4 + (16 * layer - 4 + j + 1))
                        if isinstance(e, int):
                            gu, dn = moe_w_gu[layer, e], moe_w_down[layer, e]
                        else:
                            gu = moe_w_gu[layer, bass.ds(e, 1)].rearrange("o r n -> (o r) n")
                            dn = moe_w_down[layer, bass.ds(e, 1)].rearrange("o r n -> (o r) n")
                        if k < 2:
                            load(u, rows4(gu, 4 * k, 0), 4)
                        else:
                            load(u, dn.rearrange("(k p) n -> p k n", p=P), 2)

            def late_loads(layer):
                L = late[layer]
                sp.wait_ge(s_routed, 1 + layer)
                n = sp.value_load(most[0:1, 0:1], min_val=0, max_val=T)
                with sp.If(n > PLACES):
                    sp.wait_ge(s_lo, SPLIT0[layer] + 2 * E)
                    sp.wait_ge(s_dn, 16 * layer + E)
                    with sp.Fori(0, E) as e:
                        sp.wait_ge(L["free"], e + 1)
                        gu = moe_w_gu[layer, bass.ds(e, 1)].rearrange("o r n -> (o r) n")
                        dn = moe_w_down[layer, bass.ds(e, 1)].rearrange("o r n -> (o r) n")
                        for k in range(2):
                            sp.dma_start(raw(k).rearrange("p (k n) -> p k n", k=4), rows4(gu, 4 * k, 0)
                                         ).then_inc(L["w"], 16)
                        sp.dma_start(raw(2).rearrange("p (k n) -> p k n", k=2),
                                     dn.rearrange("(k p) n -> p k n", p=P)).then_inc(L["w"], 16)
                    sp.wait_ge(L["free"], E + 1)

            expert_loads(0, 0, True)
            with sp.Fori(1, 4) as turn:
                expert_loads(0, turn, False)
            late_loads(0)
            u = 0
            order = [(cw_in, part * D + half * CG) for half in range(2) for part in (1, 2, 0)]
            order += [(cw_out, half * CG) for half in range(2)]
            for w, c0 in order:
                for kh in range(2):
                    if u < RING2:
                        if u % 3 < 2:
                            sp.wait_ge(s_lo, SPLIT0[0] + 2 * (12 + u // 3) + u % 3 + 1)
                        else:
                            sp.wait_ge(s_dn, 12 + u // 3 + 1)
                    else:
                        sp.wait_ge(s_lo, SPLIT_CONV + u - RING2 + 1)
                    load(u % RING2, rows4(w, 4 * kh, c0), 4)
                    u += 1
            expert_loads(1, 0, True)
            with sp.Fori(1, 4) as turn:
                expert_loads(1, turn, False)
            late_loads(1)

        @block.tensor
        def _(pe):
            def products(out, pairs, first, last):
                for n, (a, b) in enumerate(pairs):
                    ins = pe.matmul(out, a, b, start=first and n == 0, stop=last and n == 2)
                return ins

            def transpose_halves(stage, source, ready, after_three=None):
                for t in range(NT):
                    if t == 3 and after_three:
                        after_three()
                    ready(t)
                    for half in range(2):
                        if stage == 1 and half == 1:
                            pe.wait_ge(s_hh, 8)
                        for c in range(4):
                            f0 = (4 * half + c) * P
                            ins = pe.transpose(ps[:, 4 * half + t, c * P:(c + 1) * P],
                                               source[:, t, f0:f0 + P], ident[:, :])
                        ins.then_inc(s_tr, 1)

            def unit_features(s, kh, bank0, before_bank, count):
                for c in range(4):
                    before_bank(c)
                    for k in range(4):
                        w = slice(k * CG + c * P, k * CG + (c + 1) * P)
                        x = 4 * kh + k
                        ins = products(ps[:, bank0 + c, :],
                                       [(w_hi[:, s, w], xt_hi[:, x, :]), (w_hi[:, s, w], xt_lo[:, x, :]),
                                        (w_lo[:, s, w], xt_hi[:, x, :])],
                                       kh == 0 and k == 0, kh == 1 and k == 3)
                    if c == 3:
                        ins.then_inc(s_hl, 1)
                    elif count:
                        ins.then_inc(s_bank, 1)

            def unit_tokens(s, kh, bank0, before_bank, count):
                for t in range(NT):
                    before_bank(t)
                    tok = slice(t * P, (t + 1) * P)
                    for k in range(4):
                        w = slice(k * CG, (k + 1) * CG)
                        x = 4 * kh + k
                        ins = products(ps[:, bank0 + t, :],
                                       [(xt_hi[:, x, tok], w_hi[:, s, w]), (xt_hi[:, x, tok], w_lo[:, s, w]),
                                        (xt_lo[:, x, tok], w_hi[:, s, w])],
                                       kh == 0 and k == 0, kh == 1 and k == 3)
                    if t == 3:
                        ins.then_inc(s_hl, 1)
                    elif count:
                        ins.then_inc(s_bank, 1)

            def small_times(w_h, w_l, tok):
                for k in range(KC):
                    ins = products(ps[0:16, 0, tok],
                                   [(w_h[:, k, :], xt_hi[:, k, tok]), (w_h[:, k, :], xt_lo[:, k, tok]),
                                    (w_l[:, k, :], xt_hi[:, k, tok])], k == 0, k == KC - 1)
                return ins

            nothing = lambda c: None
            pe.wait_ge(s_const, 1)
            transpose_halves(0, x_in, lambda t: pe.wait_ge(s_x[t], 16))
            pe.wait_ge(s_small, 2)
            pe.wait_ge(s_xtl, 8)
            small_times(gate_w_hi, gate_w_lo, slice(0, T)).then_inc(s_gmm, 1)
            pe.wait_ge(s_gb, 1)
            for kind in range(4):
                ins = pe.matmul(ps[0:NH, 1 + kind, :], ident[0:16, kind * NH:(kind + 1) * NH], gates_T,
                                start=True, stop=True)
            ins.then_inc(s_grow, 1)
            pe.wait_ge(s_rows, 1)
            with pe.Fori(0, 2) as half:
                for g in range(4):
                    for kh in range(2):
                        pe.wait_ge(s_lo, half * 8 + (2 * g + kh + 1))
                        if kh == 0:
                            wait = lambda c, g=g: pe.wait_ge(s_free, half * 16 + (4 * g + c + 1))
                        else:
                            wait = nothing
                        (unit_features if g < 2 else unit_tokens)(kh, kh, 4 * (g % 2), wait, kh == 1)

            pe.wait_ge(s_rowsd, 1)
            pe.wait_ge(s_free, BANK_CREDIT + 32)
            for q, rows in enumerate((rows_a, rows_i)):
                for r in range(2):
                    for t in range(NT):
                        at = ((q * 2 + r) * NT + t) * NH
                        ins = pe.transpose(ps[:, 7, at:at + NH], rows[:, r, t * P:(t + 1) * P], ident[0:NH, 0:NH])
            ins.then_inc(s_colmm, 1)

            def head_scores(hb):
                b, h = divmod(hb, NH)
                tok = slice(b * S, (b + 1) * S)
                if hb >= 2:
                    pe.wait_ge(s_e, hb - 1)
                for r in range(2):
                    ins = pe.matmul(ps[:, 2 + hb % 2, r * S:(r + 1) * S], pick_head[:, h, :], rows_l[:, r, tok],
                                    start=True, stop=True)
                ins.then_inc(s_mb, 1)
                if hb >= 2:
                    pe.wait_ge(s_p, hb - 1)
                for j in range(2):
                    for dc in range(2):
                        ins = pe.matmul(ps[:, hb % 2, j * S:(j + 1) * S],
                                        kT[:, 2 * h + dc, b * S + j * P:b * S + (j + 1) * P],
                                        qT[:, 2 * h + dc, tok], start=dc == 0, stop=dc == 1)
                ins.then_inc(s_st, 1)

            def head_values(hb):
                b, h = divmod(hb, NH)
                p = probs[:, hb % 2, :]
                pe.wait_ge(s_p, hb + 1)
                if hb:
                    pe.wait_ge(s_hh, hb)
                else:
                    pe.wait_ge(s_cols, 1)
                sums = [[(p[:, 0:128], 0)], [(p[:, 128:256], 0), (p[:, 256:384], 1)],
                        [(p[:, 384:512], 0), (p[:, 512:640], 1)], [(p[:, 640:768], 1)]]
                for n, terms in enumerate(sums):
                    for m, (w, j) in enumerate(terms):
                        ins = pe.matmul(ps[:, 4 + n, 0:HD + 1], w, v_ext[:, 2 * b + j, h, 0:HD + 1],
                                        start=m == 0, stop=m == len(terms) - 1)
                ins.then_inc(s_av, 1)

            pe.wait_ge(s_const, 2)
            head_scores(0)
            for hb in range(8):
                if hb < 7:
                    head_scores(hb + 1)
                head_values(hb)

            def out_projection(first_unit):
                for half in range(2):
                    for kh in range(2):
                        n = first_unit + 2 * half + kh
                        pe.wait_ge(s_lo, n + 1)
                        unit_tokens(kh, kh, 4 * half, nothing, kh == 1)

            transpose_halves(1, o_sig, lambda t: pe.wait_ge(s_y, t + 1))
            pe.wait_ge(s_xtl, 16)
            out_projection(16)

            def router_half(layer, half):
                pe.wait_ge(s_small, 4)
                pe.wait_ge(s_xtl, 8 * (2 + 2 * layer) + 4 * half + 4)
                return small_times(rout_w_hi, rout_w_lo, slice(half * S, (half + 1) * S))

            def router(layer):
                router_half(layer, 1).then_inc(s_lg, 1)
                pe.wait_ge(s_lb, layer + 1)
                for t in range(NT):
                    ins = pe.transpose(ps[:, 2, t * E:(t + 1) * E], logits_T[:, t * P:(t + 1) * P],
                                       ident[0:E, 0:E])
                ins.then_inc(s_lt, 1)
                pe.wait_ge(s_chosen, layer + 1)
                out = ps[:, 1, 0:(NT + 1) * E]
                pe.matmul(out, earlier[:, :], slots(NT), start=True, stop=False)
                for back in range(1, NT + 1):
                    ins = pe.matmul(out, all_ones[:, :], slots(NT - back), start=False, stop=back == NT)
                ins.then_inc(s_rank, 1)

            def slots(first):
                return chosen_pad[:, first:first + NT + 1, :].rearrange("p s e -> p (s e)")

            def experts(layer):
                c0 = E * layer

                def rows_mm(e, j):
                    pe.wait_ge(s_oh, e + (c0 + 1))
                    if not isinstance(e, int) or e >= 1:
                        pe.wait_ge(s_ix, e + c0)
                    for t in range(NT):
                        rhs = values[:, t, e, :] if isinstance(e, int) else \
                            values[:, t, bass.ds(e, 1), :].rearrange("p o n -> p (o n)")
                        ins = pe.matmul(ps[:, 7, 0:2], one_hot[:, j % 2, t, :], rhs,
                                        start=t == 0, stop=t == NT - 1)
                    ins.then_inc(s_ixm, 1)

                def tokens_T(e, j):
                    pe.wait_ge(s_gat[j % 2], 16 * ((E // 2) * layer) + gathers(e, j))
                    if not isinstance(e, int) or e >= 1:
                        pe.wait_ge(s_glo, e + c0)
                    for c in range(KC):
                        ins = pe.transpose(ps[:, c // 4, (c % 4) * P:(c % 4 + 1) * P],
                                           xg[:, j % 2, c * P:(c + 1) * P], ident[:, :])
                    ins.then_inc(s_gtr, 1)

                def gate_up(e, j):
                    pe.wait_ge(s_glo, e + (c0 + 1))
                    if not isinstance(e, int) or e >= 2:
                        pe.wait_ge(s_h, e + (c0 - 1))
                    for kh in range(2):
                        pe.wait_ge(s_lo, e * 2 + (SPLIT0[layer] + kh + 1))
                        tok = slice((j % 2) * P, (j % 2 + 1) * P)
                        for k in range(4):
                            w = slice(k * CG, (k + 1) * CG)
                            x = 4 * kh + k
                            ins = products(ps[:, 2 + j % 2, :],
                                           [(xt_hi[:, x, tok], w_hi[:, kh, w]), (xt_hi[:, x, tok], w_lo[:, kh, w]),
                                            (xt_lo[:, x, tok], w_hi[:, kh, w])],
                                           kh == 0 and k == 0, kh == 1 and k == 3)
                        ins.then_inc(s_hl, 1)

                def hidden_T(e, j):
                    pe.wait_ge(s_h, e + (c0 + 1))
                    if not isinstance(e, int) or e >= 1:
                        pe.wait_ge(s_ht, e + c0)
                    for k in range(2):
                        ins = pe.transpose(ps[:, 4, k * P:(k + 1) * P], h_tok[:, j % 2, k * P:(k + 1) * P],
                                           ident[:, :])
                    ins.then_inc(s_htr, 1)

                def down(e, j, turn):
                    pe.wait_ge(s_ht, e + (c0 + 1))
                    pe.wait_ge(s_raw[3 * j + 2], raw_count(1 + 2 * layer, 3 * j + 2, turn))
                    if not isinstance(e, int) or e >= 1:
                        pe.wait_ge(s_ye, e + c0)
                    for half in range(2):
                        for k in range(2):
                            ins = pe.matmul(ps[:, 5 + half, :], h_T[:, j % 2, k, :],
                                            raw(3 * j + 2)[:, k * D + half * CG:k * D + (half + 1) * CG],
                                            start=k == 0, stop=k == 1)
                    ins.then_inc(s_dn, 1)

                def gathers(e, j):
                    return (e - (j % 2)) * 8 + 16

                def step(e, j, turn, left):
                    hidden_T(e, j)
                    if left > 2:
                        tokens_T(e + 2, (j + 2) % 4)
                    if left > 1:
                        gate_up(e + 1, (j + 1) % 4)
                    if left > 4:
                        rows_mm(e + 4, j)
                    down(e, j, turn)

                for e in range(3):
                    rows_mm(e, e)
                tokens_T(0, 0)
                rows_mm(3, 3)
                tokens_T(1, 1)
                gate_up(0, 0)
                with pe.Fori(0, 3) as turn:
                    for j in range(4):
                        step(turn * 4 + j, j, turn, 9)
                for j in range(4):
                    step(12 + j, j, 3, 4 - j)

            def late_experts(layer):
                L = late[layer]
                n = pe.value_load(most[0:1, 0:1], min_val=0, max_val=T)
                with pe.If(n > PLACES):
                    pe.wait_ge(s_ye, E * layer + E)
                    pe.nop().then_inc(L["free"], 1)
                    with pe.Fori(0, E) as e:
                        pe.wait_ge(L["w"], e * 48 + 48)
                        for r in range(1, ROUNDS):
                            n = e * (ROUNDS - 1) + r
                            pe.wait_ge(L["oh"], n)
                            for t in range(NT):
                                ins = pe.matmul(ps[:, 7, 0:2], one_hot[:, 0, t, :],
                                                values[:, t, bass.ds(e, 1), :].rearrange("p o n -> p (o n)"),
                                                start=t == 0, stop=t == NT - 1)
                            ins.then_inc(L["ixm"], 1)
                            pe.wait_ge(L["gat"], n * 16)
                            for c in range(KC):
                                ins = pe.transpose(ps[:, c // 4, (c % 4) * P:(c % 4 + 1) * P],
                                                   xg[:, 0, c * P:(c + 1) * P], ident[:, :])
                            ins.then_inc(L["tr"], 1)
                            pe.wait_ge(L["xt"], n)
                            for k in range(KC):
                                ins = pe.matmul(ps[:, 2, :], late_xT[:, k, :],
                                                raw(k // 4)[:, (k % 4) * CG:(k % 4 + 1) * CG],
                                                start=k == 0, stop=k == KC - 1)
                            ins.then_inc(L["gu"], 1)
                            pe.wait_ge(L["h"], n)
                            for k in range(2):
                                ins = pe.transpose(ps[:, 4, k * P:(k + 1) * P], h_tok[:, 0, k * P:(k + 1) * P],
                                                   ident[:, :])
                            ins.then_inc(L["htr"], 1)
                            pe.wait_ge(L["ht"], n)
                            for half in range(2):
                                for k in range(2):
                                    ins = pe.matmul(ps[:, 5 + half, :], h_T[:, 0, k, :],
                                                    raw(2)[:, k * D + half * CG:k * D + (half + 1) * CG],
                                                    start=k == 0, stop=k == 1)
                            ins.then_inc(L["dn"], 1)
                            pe.wait_ge(L["ye"], n)
                        pe.nop().then_inc(L["free"], 1)

            transpose_halves(2, z, lambda t: pe.wait_ge(s_xr, t + 1), lambda: router_half(0, 0))
            router(0)
            experts(0)
            late_experts(0)
            transpose_halves(3, z, lambda t: pe.wait_ge(s_xr, 4 + t + 1))
            pe.wait_ge(s_cwl, 16)
            pe.wait_ge(s_xtl, 32)
            pe.transpose(ps[:, 7, 0:3 * KC], conv_rows[:, :], ident[0:3 * KC, 0:3 * KC]).then_inc(s_cwt, 1)
            pe.wait_ge(s_taps, 1)
            with pe.Fori(0, 2) as half:
                for g in range(3):
                    for kh in range(2):
                        pe.wait_ge(s_lo, half * 6 + (SPLIT_CONV + 2 * g + kh + 1))
                        wait = nothing
                        if kh == 0 and g == 0:
                            wait = lambda c: pe.wait_ge(s_hev, half * 8 + (c + 1))
                        if kh == 0 and g == 2:
                            wait = lambda c: pe.wait_ge(s_cev, half * 4 + (c + 1))
                        unit_features(kh, kh, 4 * (g % 2), wait, kh == 1)
            pe.wait_ge(s_glx, KC)
            out_projection(SPLIT_CONV + 12)
            transpose_halves(4, z, lambda t: pe.wait_ge(s_xr, 8 + t + 1), lambda: router_half(1, 0))
            router(1)
            experts(1)
            late_experts(1)

        @block.scalar
        def _(act):
            def unit_hi(n, slot, loaded, parity):
                act.wait_ge(s_raw[slot], loaded)
                act.wait_ge(s_hl, n + 1)
                act.activation(w_hi[:, parity, :], raw(slot), ACT.Copy).then_inc(s_hi, 1)

            def halves_hi(stage, tiles=range(NT)):
                for t in tiles:
                    for half in range(2):
                        act.wait_ge(s_tr, 8 * stage + 2 * t + half + 1)
                        act.activation(xt_hi[:, 4 * half:4 * half + 4, t * P:(t + 1) * P],
                                       ps[:, 4 * half + t, :].rearrange("p (c s) -> p c s", c=4),
                                       ACT.Copy).then_inc(s_xth, 1)

            def norm_std(call, stage):
                for t in range(NT):
                    n = 4 * call + t
                    act.wait_ge(s_stat, n + 1)
                    act.activation(std[:, t:t + 1], mean_var[:, t, 1:2], ACT.Sqrt, bias=eps_ln[:, :]
                                   ).then_inc(s_std, 1)
                    if stage and t == 2:
                        halves_hi(stage, [0])
                if stage:
                    halves_hi(stage, [1, 2, 3])

            halves_hi(0)
            act.wait_ge(s_par, 64)
            act.activation(gate_w_hi[:, :, :], gate_w[:, :, :], ACT.Copy).then_inc(s_act, 1)
            act.activation(rout_w_hi[:, :, :], rout_w[:, :, :], ACT.Copy).then_inc(s_act, 1)
            for u in range(2):
                unit_hi(u, u, raw_count(0, u), u)
            act.wait_ge(s_soft, 1)
            act.activation(rows_l, rows_l, ACT.Exp).then_inc(s_soft, 1)
            act.wait_ge(s_soft, 2)
            act.activation(rows_l, rows_l, ACT.Ln, bias=1.0).then_inc(s_soft, 1)
            with act.Fori(0, 2) as half:
                for g in range(4):
                    for kh in range(2):
                        u = 2 * g + kh + 2
                        unit_hi(half * 8 + u, u % RING1, raw_count(0, u, half * 2), kh)
                    for c in range(4):
                        wait_bank(act, half * 4 + g, half * 8 + (2 * g + 1), c)
                        bank = ps[:, 4 * (g % 2) + c, :]
                        if g == 0:
                            dst = qT[:, bass.ds(half * 4 + c, 1), :].rearrange("p o t -> p (o t)")
                            act.activation(dst, bank, ACT.Copy).then_inc(s_free, 1)
                        elif g == 1:
                            dst = kT[:, bass.ds(half * 4 + c, 1), :].rearrange("p o t -> p (o t)")
                            act.activation(dst, bank, ACT.Copy, scale=HD ** -0.5).then_inc(s_free, 1)
                        elif g == 2:
                            act.activation(v_ext[:, c, bass.ds(half * 2, 2), 0:HD],
                                           bank.rearrange("p (h d) -> p h d", h=2), ACT.Copy).then_inc(s_free, 1)
                        else:
                            act.activation(o_sig[:, c, bass.ds(half * CG, CG)], bank, ACT.Sigmoid
                                           ).then_inc(s_free, 1)
            act.wait_ge(s_cols, 1)
            act.activation(exp_neg_m[:, :, :, :], cols[:, 1], ACT.Exp, scale=-1.0).then_inc(s_em, 1)

            def head_exp(hb):
                act.wait_ge(s_e, hb + 1)
                act.activation(exps[:, hb % 2, :], exps[:, hb % 2, :], ACT.Exp).then_inc(s_exp, 1)

            def forward_scale(hb):
                b, h = divmod(hb, NH)
                act.wait_ge(s_rec, hb + 1)
                for it in range(2):
                    act.activation(qT[:, 2 * h + it, b * S:(b + 1) * S], ps[:, 4 + it, 0:HD], ACT.Copy,
                                   scale=den_rec[:, hb, it:it + 1]).then_inc(s_fwd, 1)

            act.wait_ge(s_const, 2)
            head_exp(0)
            for hb in range(8):
                if hb < 7:
                    head_exp(hb + 1)
                forward_scale(hb)
                if hb == 3 or hb == 7:
                    act.wait_ge(s_hh, hb + 1)
                    act.activation(head_std[:, hb - 3:hb + 1, :], head_mv[:, hb - 3:hb + 1, :, 1], ACT.Sqrt,
                                   bias=eps_head[:, :]).then_inc(s_hstd, 1)
            halves_hi(1)
            for n in (18, 19):
                unit_hi(n, n % RING1, raw_count(0, n), n % 2)
            norm_std(0, 2)

            def router_exp(layer):
                for t in range(NT):
                    act.wait_ge(s_rlog, NT * layer + t + 1)
                    act.activation(r_prob[:, t, :], r_log[:, t, :], ACT.Exp, accum_out=r_sum[:, t:t + 1]
                                   ).then_inc(s_rexp, 1)

            def experts(layer):
                c0 = E * layer

                def gathered_hi(e, j):
                    act.wait_ge(s_gtr, e + (c0 + 1))
                    act.activation(xt_hi[:, :, (j % 2) * P:(j % 2 + 1) * P],
                                   ps[:, 0:2, :].rearrange("p b (c s) -> p (b c) s", c=4), ACT.Copy
                                   ).then_inc(s_ghi, 1)

                def silu(e, j):
                    act.wait_ge(s_hl, e * 2 + (SPLIT0[layer] + 2 + HL_CREDIT))
                    act.activation(silu_g[:, j % 2, :], ps[:, 2 + j % 2, 0:FE], ACT.Silu).then_inc(s_silu, 1)

                def hidden_read(e, j):
                    act.wait_ge(s_htr, e + (c0 + 1))
                    act.activation(h_T[:, j % 2].rearrange("p k s -> p (k s)"), ps[:, 4, 0:2 * P], ACT.Copy
                                   ).then_inc(s_ht, 1)

                def result_read(e, j):
                    act.wait_ge(s_dn, e + (c0 + 1))
                    if not isinstance(e, int) or e >= 2:
                        act.wait_ge(s_sca[j % 2], (e - (j % 2)) * 8 + 16 * (E // 2) * layer)
                    act.activation(ye[:, j % 2, :], ps[:, 5:7, :].rearrange("p b n -> p (b n)"), ACT.Copy
                                   ).then_inc(s_ye, 1)

                def units(e, j, turn, kh):
                    unit_hi(e * 2 + (SPLIT0[layer] + kh), 3 * j + kh, raw_count(1 + 2 * layer, 3 * j + kh, turn), kh)

                def step(e, j, turn, left):
                    hidden_read(e, j)
                    if left > 2:
                        gathered_hi(e + 2, (j + 2) % 4)
                        units(e + 2, (j + 2) % 4, turn + (1 if j >= 2 else 0), 0)
                    if left > 1:
                        silu(e + 1, (j + 1) % 4)
                    if left > 2:
                        units(e + 2, (j + 2) % 4, turn + (1 if j >= 2 else 0), 1)
                    result_read(e, j)

                units(0, 0, 0, 0)
                units(0, 0, 0, 1)
                gathered_hi(0, 0)
                gathered_hi(1, 1)
                units(1, 1, 0, 0)
                silu(0, 0)
                units(1, 1, 0, 1)
                for j in range(4):
                    step(j, j, 0, 9)
                with act.Fori(1, 3) as turn:
                    for j in range(4):
                        step(turn * 4 + j, j, turn, 9)
                for j in range(4):
                    step(12 + j, j, 3, 4 - j)

            def late_experts(layer):
                L = late[layer]
                n = act.value_load(most[0:1, 0:1], min_val=0, max_val=T)
                with act.If(n > PLACES):
                    act.wait_ge(s_sca[0], 16 * (E // 2) * (layer + 1))
                    with act.Fori(0, E) as e:
                        for r in range(1, ROUNDS):
                            n = e * (ROUNDS - 1) + r
                            act.wait_ge(L["tr"], n)
                            act.activation(late_xT.rearrange("p c s -> p (c s)"),
                                           ps[:, 0:2, :].rearrange("p b n -> p (b n)"), ACT.Copy).then_inc(L["xt"], 1)
                            act.wait_ge(L["gu"], n)
                            act.activation(silu_g[:, 0, :], ps[:, 2, 0:FE], ACT.Silu).then_inc(L["silu"], 1)
                            act.wait_ge(L["htr"], n)
                            act.activation(h_T[:, 0].rearrange("p k s -> p (k s)"), ps[:, 4, 0:2 * P], ACT.Copy
                                           ).then_inc(L["ht"], 1)
                            act.wait_ge(L["dn"], n)
                            act.activation(ye[:, 0, :], ps[:, 5:7, :].rearrange("p b n -> p (b n)"), ACT.Copy
                                           ).then_inc(L["ye"], 1)
                            act.wait_ge(L["sca"], n * 16)

            def scale_residual(call):
                for t in range(NT):
                    act.wait_ge(s_res[t], 16 * (call + 1))
                    act.activation(z[:, t, :], z[:, t, :], ACT.Copy, scale=ALPHA).then_inc(s_ax, 1)

            router_exp(0)
            experts(0)
            late_experts(0)
            scale_residual(1)
            norm_std(1, 3)
            for u in range(2):
                unit_hi(SPLIT_CONV + u, u, raw_count(2, u), u)
            with act.Fori(0, 2) as half:
                for g in range(3):
                    for kh in range(2):
                        u = 2 * g + kh + 2
                        unit_hi(half * 6 + (SPLIT_CONV + u), u % RING2, raw_count(2, u, half), kh)
                    if g == 0:
                        for c in range(4):
                            wait_bank(act, half * 3 + 10, half * 6 + (SPLIT_CONV + 1), c)
                            act.activation(c_T[:, c, :], ps[:, c, :], ACT.Copy).then_inc(s_cev, 1)
            for c in range(KC):
                act.wait_ge(s_conv, 4 * (c // 4 + 1))
                act.wait_ge(s_hl, SPLIT_CONV + 12 + HL_CREDIT)
                act.activation(xt_hi[:, c, :], g_T[:, c, :], ACT.Copy).then_inc(s_ghx, 1)
            for n in (14, 15):
                unit_hi(SPLIT_CONV + n, n % RING2, raw_count(2, n), n % 2)
            norm_std(2, 4)
            router_exp(1)
            experts(1)
            late_experts(1)
            scale_residual(3)
            norm_std(3, 0)

        @block.vector
        def _(dve):
            step_done = Steps(dve, s_dve)

            def do(ins):
                step_done(ins)
                step_done.wait()

            def unit_lo(n, slot, parity):
                dve.wait_ge(s_hi, n + 1)
                dve.tensor_tensor(w_lo[:, parity, :], raw(slot), w_hi[:, parity, :].bitcast(F32), ALU.subtract
                                  ).then_inc(s_lo, 1)

            def half_lo(stage, t):
                for half in range(2):
                    dve.wait_ge(s_xth, 8 * stage + 2 * t + half + 1)
                    hb = xt_hi[:, 4 * half:4 * half + 4, t * P:(t + 1) * P]
                    dve.tensor_tensor(xt_lo[:, 4 * half:4 * half + 4, t * P:(t + 1) * P],
                                      ps[:, 4 * half + t, :].rearrange("p (c s) -> p c s", c=4),
                                      hb.bitcast(F32), ALU.subtract).then_inc(s_xtl, 1)

            def norm(call, stage, sum_tile):
                def stat(t):
                    sum_tile(t)
                    for hf in range(2):
                        step_done(dve.bn_stats(stats[:, t, hf, :], z[:, t, hf * CG:(hf + 1) * CG]))
                    step_done.wait()
                    dve.bn_aggr(mean_var[:, t, :], stats[:, t, :, :].rearrange("p a b -> p (a b)")
                                ).then_inc(s_stat, 1)

                def scale(t):
                    n = 4 * call + t
                    dve.wait_ge(s_std, n + 1)
                    do(dve.reciprocal(rstd[:, t:t + 1], std[:, t:t + 1]))
                    do(dve.tensor_scalar(z[:, t, :], z[:, t, :], mean_var[:, t, 0:1], rstd[:, t:t + 1],
                                         ALU.subtract, ALU.mult))
                    if t == 0:
                        dve.wait_ge(s_lnp, 16 + 32 * (call + 1))
                    dve.tensor_tensor(z[:, t, :], z[:, t, :], ln_g[:, :], ALU.mult).then_inc(s_zn, 1)

                stat(0)
                stat(1)
                scale(0)
                stat(2)
                scale(1)
                if stage:
                    half_lo(stage, 0)
                stat(3)
                scale(2)
                if stage:
                    half_lo(stage, 1)
                scale(3)
                if stage:
                    half_lo(stage, 2)
                    half_lo(stage, 3)

            dve.engine_nop().then_inc(s_hl, HL_CREDIT)
            dve.engine_nop().then_inc(s_free, BANK_CREDIT)
            dve.engine_nop().then_inc(s_hev, 4)
            dve.memset(v_ext[:, :, :, HD:VW], 1.0).then_inc(s_dve, 1)
            step_done.n += 1
            for t in range(NT):
                half_lo(0, t)
            dve.wait_ge(s_act, 1)
            dve.tensor_tensor(gate_w_lo[:, :, :], gate_w[:, :, :], gate_w_hi[:, :, :].bitcast(F32), ALU.subtract
                              ).then_inc(s_small, 2)
            for u in range(2):
                unit_lo(u, u, u)
            dve.wait_ge(s_gmm, 1)
            dve.tensor_scalar(gates_T, ps[0:16, 0, :], gate_b[:, :], None, ALU.add).then_inc(s_gb, 1)
            dve.wait_ge(s_grow, 1)
            do(dve.tensor_copy(rows_f, ps[0:NH, 2:5:2, :]))
            dve.tensor_copy(rows_i, ps[0:NH, 1:4:2, :]).then_inc(s_rows, 1)
            dve.scalar_tensor_tensor(out=rows_l, in0=rows_f, scalar=-1.0, in1=rows_f, op0=ALU.mult, op1=ALU.min
                                     ).then_inc(s_soft, 1)
            dve.wait_ge(s_act, 2)
            dve.tensor_tensor(rout_w_lo[:, :, :], rout_w[:, :, :], rout_w_hi[:, :, :].bitcast(F32), ALU.subtract
                              ).then_inc(s_small, 2)
            dve.wait_ge(s_soft, 3)
            do(dve.scalar_tensor_tensor(out=rows_f, in0=rows_f, scalar=0.0, in1=rows_l, op0=ALU.min,
                                        op1=ALU.subtract))
            def along(rows, r, b):
                part = rows[:, r, b * S:(b + 1) * S]
                return part[:, ::-1] if r else part
            for r in range(2):
                for b in range(2):
                    step_done(dve.tensor_tensor_scan(along(rows_c, r, b), along(rows_f, r, b), along(rows_f, r, b),
                                                     0.0, ALU.add, ALU.bypass))
            step_done.wait()
            dve.wait_ge(s_rows, 1)
            do(dve.tensor_tensor(rows_a, rows_i, rows_c, ALU.subtract))
            for r in range(2):
                for b in range(2):
                    step_done(dve.tensor_tensor_scan(along(rows_m, r, b), along(rows_a, r, b), along(rows_a, r, b),
                                                     NEG, ALU.max, ALU.bypass))
            step_done.wait()
            do(dve.tensor_tensor(rows_i, rows_c, rows_m, ALU.add))
            dve.tensor_scalar(rows_l, rows_m, -1.0, None, ALU.mult).then_inc(s_rowsd, 1)
            with dve.Fori(0, 2) as half:
                for g in range(4):
                    for kh in range(2):
                        u = 2 * g + kh + 2
                        unit_lo(half * 8 + u, u % RING1, kh)
            dve.wait_ge(s_colmm, 1)
            dve.tensor_copy(cols[:, :, :, :, :].rearrange("p a r t h -> p (a r t h)"), ps[:, 7, 0:64]
                            ).then_inc(s_cols, 1)
            dve.wait_ge(s_cols, 1)

            def head_exponents(hb):
                b, h = divmod(hb, NH)
                dve.wait_ge(s_mb, hb + 1)
                if hb >= 2:
                    dve.wait_ge(s_p, hb - 1)
                else:
                    dve.wait_ge(s_rowsd, 1)
                x, m = exps[:, hb % 2, :], ps[:, 2 + hb % 2, :]
                a = lambda r, j: cols[:, 0, r, 2 * b + j, h:h + 1]
                for out, spread, col, mask in (
                        (x[:, 0:256], m[:, 0:256], a(0, 0), mask_fw[:, 0:256]),
                        (x[:, 256:384], m[:, 128:256], a(0, 1), mask_fw[:, 0:128]),
                        (x[:, 384:512], m[:, 256:384], a(1, 0), mask_bw[:, 128:256]),
                        (x[:, 512:768], m[:, 256:512], a(1, 1), mask_bw[:, 0:256])):
                    ins = dve.scalar_tensor_tensor(out=out, in0=spread, scalar=col, in1=mask, op0=ALU.add,
                                                   op1=ALU.min)
                ins.then_inc(s_e, 1)

            def head_weights(hb):
                dve.wait_ge(s_exp, hb + 1)
                dve.wait_ge(s_st, hb + 1)
                if hb >= 2:
                    dve.wait_ge(s_av, hb - 1)
                x, w, s = exps[:, hb % 2, :], probs[:, hb % 2, :], ps[:, hb % 2, :]
                for at, n, sc in ((0, 256, 0), (256, 128, 384), (384, 128, 0), (512, 256, 256)):
                    ins = dve.tensor_tensor(w[:, at:at + n], s[:, sc:sc + n], x[:, at:at + n], ALU.mult)
                ins.then_inc(s_p, 1)

            def head_out(hb):
                b, h = divmod(hb, NH)
                dve.wait_ge(s_av, hb + 1)
                do(dve.tensor_copy(den[:, :], ps[:, 4:8, HD]))
                do(dve.scalar_tensor_tensor(out=den_neg[:, :], in0=den[:, :], scalar=-1.0, in1=den[:, :],
                                            op0=ALU.mult, op1=ALU.max))
                if hb == 0:
                    dve.wait_ge(s_em, 1)
                do(dve.tensor_tensor(den[:, :].rearrange("p (r t) -> p r t", r=2),
                                     den_neg[:, :].rearrange("p (r t) -> p r t", r=2),
                                     exp_neg_m[:, :, 2 * b:2 * b + 2, h], ALU.max))
                dve.reciprocal(den_rec[:, hb, :], den[:, :]).then_inc(s_rec, 1)
                dve.wait_ge(s_rec, hb + 1)
                for it in range(2):
                    out = qT[:, 2 * h + it, b * S:(b + 1) * S]
                    dve.wait_ge(s_fwd, 2 * hb + it + 1)
                    do(dve.scalar_tensor_tensor(out=out, in0=ps[:, 6 + it, 0:HD], scalar=den_rec[:, hb, 2 + it:3 + it],
                                                in1=out, op0=ALU.mult, op1=ALU.add))
                    do(dve.bn_stats(head_stats[:, hb, it, :], out))
                    ins = dve.bn_aggr(head_mv[:, hb, it, :], head_stats[:, hb, it, :])
                    if it == 0:
                        step_done(ins)
                ins.then_inc(s_hh, 1)

            def request_out(b):
                dve.wait_ge(s_hstd, b + 1)
                do(dve.reciprocal(head_rstd[:, 4 * b:4 * b + 4, :], head_std[:, 4 * b:4 * b + 4, :]))
                for it in range(2):
                    t = 2 * b + it
                    for h in range(NH):
                        part = qT[:, 2 * h + it, b * S:(b + 1) * S]
                        step_done(dve.tensor_scalar(part, part, head_mv[:, 4 * b + h, it, 0:1],
                                                    head_rstd[:, 4 * b + h, it:it + 1], ALU.subtract, ALU.mult))
                    step_done.wait()
                    dve.wait_ge(s_og, t + 1)
                    o = o_sig[:, t, :].rearrange("p (h d) -> p h d", h=NH)
                    dve.tensor_tensor(o, o, qT[:, it:8:2, b * S:(b + 1) * S], ALU.mult).then_inc(s_y, 1)

            dve.wait_ge(s_const, 2)
            head_exponents(0)
            for hb in range(8):
                if hb < 7:
                    head_exponents(hb + 1)
                head_weights(hb)
                if hb:
                    head_out(hb - 1)
                if hb == 5:
                    request_out(0)
            head_out(7)
            request_out(1)
            for t in range(NT):
                half_lo(1, t)
            for n in (18, 19):
                unit_lo(n, n % RING1, n % 2)

            def mixer_sum(call, group, unit):
                def f(t):
                    wait_bank(dve, group, unit, t)
                    dve.wait_ge(s_res[t], 16 * (call + 1))
                    for half in range(2):
                        zt = z[:, t, half * CG:(half + 1) * CG]
                        step_done(dve.scalar_tensor_tensor(out=zt, in0=zt, scalar=ALPHA, in1=ps[:, 4 * half + t, :],
                                                           op0=ALU.mult, op1=ALU.add))
                    step_done.wait()
                return f

            def expert_sum(call):
                def f(t):
                    n = NT * (call // 2) + t
                    dve.wait_ge(s_ax, n + 1)
                    dve.wait_ge(s_yb[t % 2], 32 * (n // 2 + 1))
                    do(dve.scalar_tensor_tensor(out=z[:, t, :], in0=y_back[:, t % 2, 0, :], scalar=gate_of[:, t, 0:1],
                                                in1=z[:, t, :], op0=ALU.mult, op1=ALU.add))
                    dve.scalar_tensor_tensor(out=z[:, t, :], in0=y_back[:, t % 2, 1, :], scalar=gate_of[:, t, 1:2],
                                             in1=z[:, t, :], op0=ALU.mult, op1=ALU.add).then_inc(s_sum2, 1)
                    dve.wait_ge(s_sum2, n + 1)
                return f

            def first_where(out, mask, order):
                do(dve.tensor_tensor(r_b_view(out), mask, order, ALU.mult))
                do(dve.tensor_reduce(r_one[:, :], r_b_view(out), AX.X, ALU.max))
                do(dve.tensor_tensor(out, r_b_view(out), r_one[:, :].unsqueeze(2).to_broadcast(list(out.shape)),
                                     ALU.is_equal))

            def r_b_view(out):
                return r_b[:, :, 0:out.shape[2]]

            def choose(layer):
                wide = lambda a, n: a.unsqueeze(2).to_broadcast([P, NT, n])
                dve.wait_ge(s_lg, layer + 1)
                dve.tensor_scalar(logits_T, ps[0:E, 0, :], rout_b[:, :], None, ALU.add).then_inc(s_lb, 1)
                dve.wait_ge(s_lt, layer + 1)
                logits = ps[:, 2, 0:NT * E].rearrange("p (t e) -> p t e", t=NT)
                do(dve.tensor_reduce(r_one[:, :], logits, AX.X, ALU.max))
                dve.tensor_tensor(r_log[:, :, :], logits, wide(r_one[:, :], E), ALU.subtract
                                  ).then_inc(s_rlog, NT)
                dve.wait_ge(s_rexp, NT * (layer + 1))
                do(dve.reciprocal(r_one[:, :], r_sum[:, :]))
                do(dve.tensor_tensor(r_prob[:, :, :], r_prob[:, :, :], wide(r_one[:, :], E), ALU.mult))
                g = r_prob[:, :, :].rearrange("p t (g e) -> p (t g) e", g=NG)
                step_done(dve.tensor_tensor(r_pair[:, :, 0:3], g[:, :, 0:3], g[:, :, 1:4], ALU.add))
                step_done(dve.tensor_tensor(r_pair[:, :, 3:5], g[:, :, 0:2], g[:, :, 2:4], ALU.add))
                do(dve.tensor_tensor(r_pair[:, :, 5:6], g[:, :, 0:1], g[:, :, 3:4], ALU.add))
                do(dve.tensor_reduce(r_score[:, :, :].rearrange("p t g -> p (t g)"), r_pair[:, :, :], AX.X, ALU.max))
                do(dve.tensor_reduce(r_one[:, :], r_score[:, :, :], AX.X, ALU.max))
                do(dve.tensor_tensor(r_group[:, :, :], r_score[:, :, :], wide(r_one[:, :], NG), ALU.is_equal))
                first_where(r_group[:, :, :], r_group[:, :, :],
                            group_first[:, :].unsqueeze(1).to_broadcast([P, NT, NG]))
                in_group = r_group[:, :, :].rearrange("p t g -> p (t g)").unsqueeze(2).to_broadcast([P, NT * NG, GE])
                grouped = lambda a: a[:, :, :].rearrange("p t (g e) -> p (t g) e", g=NG)
                do(dve.tensor_tensor(grouped(r_a), grouped(r_prob), in_group, ALU.mult))
                do(dve.tensor_scalar(grouped(r_log), in_group, -1.0, None, ALU.add))
                do(dve.tensor_tensor(r_a[:, :, :], r_a[:, :, :], r_log[:, :, :], ALU.add))
                order = expert_first[:, :].unsqueeze(1).to_broadcast([P, NT, E])
                do(dve.tensor_reduce(r_v1[:, :], r_a[:, :, :], AX.X, ALU.max))
                do(dve.tensor_tensor(is_top1[:, :, :], r_a[:, :, :], wide(r_v1[:, :], E), ALU.is_equal))
                first_where(is_top1[:, :, :], is_top1[:, :, :], order)
                do(dve.scalar_tensor_tensor(out=r_a[:, :, :], in0=is_top1[:, :, :], scalar=-4.0, in1=r_a[:, :, :],
                                            op0=ALU.mult, op1=ALU.add))
                do(dve.tensor_reduce(r_v2[:, :], r_a[:, :, :], AX.X, ALU.max))
                do(dve.tensor_tensor(is_top2[:, :, :], r_a[:, :, :], wide(r_v2[:, :], E), ALU.is_equal))
                first_where(is_top2[:, :, :], is_top2[:, :, :], order)
                dve.tensor_tensor(chosen, is_top1[:, :, :], is_top2[:, :, :], ALU.add).then_inc(s_chosen, 1)
                dve.wait_ge(s_chosen, layer + 1)
                do(dve.tensor_tensor(r_one[:, :], r_v1[:, :], r_v2[:, :], ALU.add))
                do(dve.reciprocal(r_sum[:, :], r_one[:, :]))
                do(dve.tensor_tensor(gate_of[:, :, 0], r_v1[:, :], r_sum[:, :], ALU.mult))
                do(dve.tensor_tensor(gate_of[:, :, 1], r_v2[:, :], r_sum[:, :], ALU.mult))
                do(dve.tensor_copy(values[:, :, :, 0], wide(token_no[:, :], E)))
                do(dve.scalar_tensor_tensor(out=values[:, :, :, 1], in0=is_top2[:, :, :], scalar=float(T),
                                            in1=wide(token_no[:, :], E), op0=ALU.mult, op1=ALU.add))
                dve.wait_ge(s_rank, layer + 1)
                rank = ps[:, 1, 0:NT * E].rearrange("p (t e) -> p t e", t=NT)
                do(dve.tensor_scalar(r_a[:, :, :], rank, 1.0, None, ALU.add))
                do(dve.tensor_tensor(r_a[:, :, :], r_a[:, :, :], chosen, ALU.mult))
                do(dve.tensor_scalar(place[:, :, :], r_a[:, :, :], -1.0, None, ALU.add))
                do(dve.tensor_reduce(r_max[:, :], ps[:, 1, NT * E:(NT + 1) * E], AX.X, ALU.max))
                dve.tensor_copy(most[:, :], r_max[:, :]).then_inc(s_routed, 1)

            def at_expert(a, t, e):
                return a[:, t, e:e + 1] if isinstance(e, int) else a[:, t, bass.ds(e, 1)]

            def experts(layer):
                c0 = E * layer

                def one_hots(e, j):
                    if not isinstance(e, int) or e >= 2:
                        dve.wait_ge(s_ixm, e + (c0 - 1))
                    for t in range(NT):
                        ins = dve.tensor_scalar(one_hot[:, j % 2, t, 0:P], place_no[:, :], at_expert(place, t, e), None,
                                                ALU.is_equal)
                    ins.then_inc(s_oh, 1)

                def row_numbers(e, j):
                    dve.wait_ge(s_ixm, e + (c0 + 1))
                    dst = rows_of[:, e, :] if isinstance(e, int) else \
                        rows_of[:, bass.ds(e, 1), :].rearrange("p o n -> p (o n)")
                    dve.tensor_scalar(dst, ps[:, 7, 0:2], NO_ROW, None, ALU.add).then_inc(s_ix, 1)

                def gathered_lo(e, j):
                    dve.wait_ge(s_ghi, e + (c0 + 1))
                    dst = slice((j % 2) * P, (j % 2 + 1) * P)
                    dve.tensor_tensor(xt_lo[:, :, dst], ps[:, 0:2, :].rearrange("p b (c s) -> p (b c) s", c=4),
                                      xt_hi[:, :, dst].bitcast(F32), ALU.subtract).then_inc(s_glo, 1)

                def hidden(e, j):
                    dve.wait_ge(s_silu, e + (c0 + 1))
                    if not isinstance(e, int) or e >= 2:
                        dve.wait_ge(s_htr, e + (c0 - 1))
                    dve.tensor_tensor(h_tok[:, j % 2, :], ps[:, 2 + j % 2, FE:2 * FE], silu_g[:, j % 2, :], ALU.mult
                                      ).then_inc(s_h, 1)

                def units(e, j, kh):
                    unit_lo(e * 2 + (SPLIT0[layer] + kh), 3 * j + kh, kh)

                def step(e, j, left):
                    if left > 2:
                        gathered_lo(e + 2, (j + 2) % 4)
                    if left > 4:
                        one_hots(e + 4, j)
                    if left > 2:
                        units(e + 2, (j + 2) % 4, 0)
                    if left > 1:
                        hidden(e + 1, (j + 1) % 4)
                    if left > 4:
                        row_numbers(e + 4, j)
                    if left > 2:
                        units(e + 2, (j + 2) % 4, 1)

                dve.wait_ge(s_routed, layer + 1)
                one_hots(0, 0)
                one_hots(1, 1)
                row_numbers(0, 0)
                row_numbers(1, 1)
                one_hots(2, 2)
                row_numbers(2, 2)
                one_hots(3, 3)
                units(0, 0, 0)
                units(0, 0, 1)
                gathered_lo(0, 0)
                row_numbers(3, 3)
                gathered_lo(1, 1)
                units(1, 1, 0)
                hidden(0, 0)
                units(1, 1, 1)
                for j in range(4):
                    step(j, j, 9)
                with dve.Fori(1, 3) as turn:
                    for j in range(4):
                        step(turn * 4 + j, j, 9)
                for j in range(4):
                    step(12 + j, j, 4 - j)

            def late_experts(layer):
                L = late[layer]
                n = dve.value_load(most[0:1, 0:1], min_val=0, max_val=T)
                with dve.If(n > PLACES):
                    dve.wait_ge(s_ye, E * layer + E)
                    dve.wait_ge(s_sca[0], 16 * (E // 2) * (layer + 1))
                    dve.wait_ge(s_sca[1], 16 * (E // 2) * (layer + 1))
                    with dve.Fori(0, E) as e:
                        for r in range(1, ROUNDS):
                            n = e * (ROUNDS - 1) + r
                            for t in range(NT):
                                ins = dve.tensor_scalar(one_hot[:, 0, t, :], place_no[:, :], float(r * PLACES),
                                                        at_expert(place, t, e), ALU.add, ALU.is_equal)
                            ins.then_inc(L["oh"], 1)
                            dve.wait_ge(L["ixm"], n)
                            dve.tensor_scalar(rows_of[:, 0, :], ps[:, 7, 0:2], NO_ROW, None, ALU.add
                                              ).then_inc(L["ix"], 1)
                            dve.wait_ge(L["silu"], n)
                            dve.tensor_tensor(h_tok[:, 0, :], ps[:, 2, FE:2 * FE], silu_g[:, 0, :], ALU.mult
                                              ).then_inc(L["h"], 1)
                            dve.wait_ge(L["sca"], n * 16)

            norm(0, 2, mixer_sum(0, 9, 19))
            choose(0)
            experts(0)
            late_experts(0)
            norm(1, 3, expert_sum(1))
            dve.wait_ge(s_cwt, 1)
            dve.tensor_copy(taps[:, :, :].rearrange("p w c -> p (w c)"), ps[:, 7, 0:3 * KC]).then_inc(s_taps, 1)
            dve.wait_ge(s_taps, 1)
            for u in range(2):
                unit_lo(SPLIT_CONV + u, u, u)
            per_half = 4 * 3
            with dve.Fori(0, 2) as half:
                step_done.loop(half, per_half)
                for g in range(3):
                    for kh in range(2):
                        u = 2 * g + kh + 2
                        unit_lo(half * 6 + (SPLIT_CONV + u), u % RING2, kh)
                    for c in range(4):
                        if g == 1:
                            wait_bank(dve, half * 3 + 11, half * 6 + (SPLIT_CONV + 3), c)
                            dve.wait_ge(s_cev, half * 4 + (c + 1))
                            dve.tensor_tensor(u_T[:, c, :], ps[:, 4 + c, :], c_T[:, c, :], ALU.mult
                                              ).then_inc(s_hev, 1)
                        elif g == 2:
                            wait_bank(dve, half * 3 + 12, half * 6 + (SPLIT_CONV + 5), c)
                            dst = g_T[:, bass.ds(half * 4 + c, 1), :].rearrange("p o t -> p (o t)")
                            dve.tensor_tensor(dst, ps[:, c, :], conv_T[:, c, :], ALU.mult).then_inc(s_hev, 1)
                    if g == 1:
                        dve.wait_ge(s_hev, half * 8 + 8)
                        for c in range(4):
                            tap = lambda w: taps[:, w, bass.ds(half * 4 + c, 1)]
                            u2 = u_T[:, c, :].rearrange("p (b t) -> p b t", b=2)
                            o2 = conv_T[:, c, :].rearrange("p (b t) -> p b t", b=2)
                            do(dve.tensor_scalar(o2, u2, tap(1), None, ALU.mult))
                            do(dve.scalar_tensor_tensor(out=o2[:, :, 1:S], in0=u2[:, :, 0:S - 1], scalar=tap(0),
                                                        in1=o2[:, :, 1:S], op0=ALU.mult, op1=ALU.add))
                            do(dve.scalar_tensor_tensor(out=o2[:, :, 0:S - 1], in0=u2[:, :, 1:S], scalar=tap(2),
                                                        in1=o2[:, :, 0:S - 1], op0=ALU.mult, op1=ALU.add))
                    if g == 2:
                        dve.wait_ge(s_hev, half * 8 + 12)
                        dve.engine_nop().then_inc(s_conv, 4)
                step_done.end(2)
            for c in range(KC):
                dve.wait_ge(s_ghx, c + 1)
                dve.tensor_tensor(xt_lo[:, c, :], g_T[:, c, :], xt_hi[:, c, :].bitcast(F32), ALU.subtract
                                  ).then_inc(s_glx, 1)
            for n in (14, 15):
                unit_lo(SPLIT_CONV + n, n % RING2, n % 2)
            norm(2, 4, mixer_sum(2, 17, SPLIT_CONV + 15))
            choose(1)
            experts(1)
            late_experts(1)
            norm(3, 0, expert_sum(3))

        @block.gpsimd
        def _(pool):
            done = Steps(pool, s_pool)
            last_token, last_result = pool.to_reg(T - 1), pool.to_reg(2 * T - 1)
            x_tiles = [x_prompt[0, 0:P, :], x_prompt[0, P:S, :], x_sample[0, 0:P, :], x_sample[0, P:S, :]]
            y_tiles = [y_prompt[0, 0:P, :], y_prompt[0, P:S, :], y_sample[0, 0:P, :], y_sample[0, P:S, :]]

            def spread(row):
                return row.rearrange("(o n) -> o n", o=1).to_broadcast([P, D])

            done(pool.memset(ident[:, :], 0.0))
            done.wait()
            pool.affine_select(out=ident[:, :], in_=ident[:, :], compare_op=ALU.not_equal, fill=1.0, base=0,
                               pattern=[[-1, P]], channel_multiplier=1).then_inc(s_const, 1)
            pool.dma_start(ln_g[:, :], spread(mlstm_norm_g[0])).then_inc(s_lnp, 16)
            done(pool.memset(pick_head[:, :, :], 0.0))
            done(pool.memset(mask_fw[:, :], 0.0))
            done(pool.memset(mask_bw[:, :], 0.0))
            done(pool.memset(earlier[:, :], 0.0))
            done(pool.memset(all_ones[:, :], 1.0))
            done(pool.memset(chosen_pad[:, :, :], 0.0))
            done(pool.memset(eps_ln[:, :], LN_EPS))
            done(pool.memset(eps_head[:, :], HEAD_EPS))
            done.wait()
            done(pool.affine_select(out=pick_head[:, :, :], in_=pick_head[:, :, :], compare_op=ALU.not_equal,
                                    fill=1.0, base=0, pattern=[[1, NH], [0, P]], channel_multiplier=-1))
            done(pool.affine_select(out=mask_fw[:, :], in_=mask_fw[:, :], compare_op=ALU.is_ge, fill=NEG,
                                    base=0, pattern=[[1, S]], channel_multiplier=-1))
            done(pool.affine_select(out=mask_bw[:, :], in_=mask_bw[:, :], compare_op=ALU.is_ge, fill=NEG,
                                    base=P, pattern=[[-1, S]], channel_multiplier=1))
            done(pool.affine_select(out=earlier[:, :], in_=earlier[:, :], compare_op=ALU.is_ge, fill=1.0,
                                    base=0, pattern=[[-1, P]], channel_multiplier=1))
            done(pool.iota(place_no[:, :], pattern=[[1, P]], base=0, channel_multiplier=0,
                           allow_small_or_imprecise_dtypes=True))
            done(pool.iota(token_no[:, :], pattern=[[P, NT]], base=-int(NO_ROW), channel_multiplier=1,
                           allow_small_or_imprecise_dtypes=True))
            done(pool.iota(group_first[:, :], pattern=[[-1, NG]], base=NG, channel_multiplier=0,
                           allow_small_or_imprecise_dtypes=True))
            done(pool.iota(expert_first[:, :], pattern=[[-1, E]], base=E, channel_multiplier=0,
                           allow_small_or_imprecise_dtypes=True))
            if PLACES < P:
                done.wait()
                done(pool.affine_select(out=place_no[:, :], in_=place_no[:, :], compare_op=ALU.is_ge, fill=1e6,
                                        base=PLACES - 1, pattern=[[-1, P]], channel_multiplier=0))
            done.wait()
            pool.engine_nop().then_inc(s_const, 1)
            pool.wait_ge(s_lnp, 16)
            pool.wait_ge(s_free, BANK_CREDIT + 32)
            for t in range(NT):
                pool.tensor_tensor(o_sig[:, t, :], o_sig[:, t, :], ln_g[:, :], ALU.mult).then_inc(s_og, 1)
            pool.wait_ge(s_og, NT)

            def norm_weights(call, g, b):
                pool.dma_start(ln_g[:, :], spread(g)).then_inc(s_lnp, 16)
                pool.dma_start(ln_b[:, :], spread(b)).then_inc(s_lnp, 16)

            def residuals(call, sources):
                for t in range(NT):
                    pool.dma_start(z[:, t, :], sources[t]).then_inc(s_res[t], 16)

            def norm_end(call, targets):
                pool.wait_ge(s_lnp, 16 + 32 * (call + 1))
                for t in range(NT):
                    pool.wait_ge(s_zn, 4 * call + t + 1)
                    pool.tensor_tensor(z[:, t, :], z[:, t, :], ln_b[:, :], ALU.add).then_inc(s_xr, 1)
                    pool.wait_ge(s_xr, 4 * call + t + 1)
                    pool.dma_start(targets[t], z[:, t, :]).then_inc(s_st_x[t], 16)

            def tiles(a):
                return [a[t * P:(t + 1) * P, :] for t in range(NT)]

            def experts(layer):
                call = 2 * layer
                source, target = x_dram[call], y_dram[layer]
                for t in range(NT):
                    pool.wait_ge(s_st_x[t], 16 * (call + 1))
                pool.wait_ge(s_tr, 8 * (3 + 2 * layer))
                pool.memset(xg[:, :, :], 0.0).then_inc(s_xg0, 1)
                pool.wait_ge(s_xg0, layer + 1)
                c0 = E * layer

                def gather(e, j):
                    pool.wait_ge(s_ix, e + (c0 + 1))
                    if not isinstance(e, int) or e >= 2:
                        pool.wait_ge(s_gtr, e + (c0 - 1))
                    pool.indirect_dma_start(out=xg[:, j % 2, :], out_offset=None, in_=source,
                                            in_offset=bass.IndirectOffsetOnAxis(rows_of[:, e, 0:1], 0),
                                            bounds_check=last_token, oob_is_err=False).then_inc(s_gat[j % 2], 16)

                def scatter(e, j):
                    pool.wait_ge(s_ye, e + (c0 + 1))
                    pool.indirect_dma_start(out=target, out_offset=bass.IndirectOffsetOnAxis(rows_of[:, e, 1:2], 0),
                                            in_=ye[:, j % 2, :], in_offset=None,
                                            bounds_check=last_result, oob_is_err=False).then_inc(s_sca[j % 2], 16)

                for e in range(4):
                    gather(e, e)
                for e in range(E):
                    if e + 4 < E:
                        gather(e + 4, e % 4)
                    scatter(e, e % 4)
                for b in range(2):
                    pool.wait_ge(s_sca[b], 16 * (E // 2) * (layer + 1))

                L = late[layer]
                n = pool.value_load(most[0:1, 0:1], min_val=0, max_val=T)
                limit = pool.alloc_register()
                one_less = pool.to_reg(T - 2), pool.to_reg(2 * T - 2)
                with pool.If(n > PLACES):
                    with pool.Fori(0, E) as e:
                        for r in range(1, ROUNDS):
                            n = e * (ROUNDS - 1) + r
                            pool.wait_ge(L["ix"], n)
                            pool.reg_add(limit, one_less[0], 1)
                            pool.indirect_dma_start(out=xg[:, 0, :], out_offset=None, in_=source,
                                                    in_offset=bass.IndirectOffsetOnAxis(rows_of[:, 0, 0:1], 0),
                                                    bounds_check=limit, oob_is_err=False).then_inc(L["gat"], 16)
                            pool.wait_ge(L["ye"], n)
                            pool.reg_add(limit, one_less[1], 1)
                            pool.indirect_dma_start(out=target,
                                                    out_offset=bass.IndirectOffsetOnAxis(rows_of[:, 0, 1:2], 0),
                                                    in_=ye[:, 0, :], in_offset=None,
                                                    bounds_check=limit, oob_is_err=False).then_inc(L["sca"], 16)
                            pool.wait_ge(L["sca"], n * 16)
                residuals(call + 1, tiles(source))
                back = target.rearrange("(k t p) d -> t p k d", k=2, p=P)
                for t in range(NT):
                    n = NT * layer + t
                    if t >= 2:
                        pool.wait_ge(s_sum2, n - 1)
                    for k in range(2):
                        pool.dma_start(y_back[:, t % 2, k, :], back[t, :, k, :]).then_inc(s_yb[t % 2], 16)

            pool.wait_ge(s_e, 8)
            norm_weights(0, ln1_g[0], ln1_b[0])
            pool.wait_ge(s_mb, 8)
            residuals(0, x_tiles)
            norm_end(0, tiles(x_dram[0]))
            pool.wait_ge(s_zn, 4)
            norm_weights(1, ln2_g[0], ln2_b[0])
            experts(0)
            pool.dma_start(conv_rows, conv_w[0].rearrange("w (c p) -> (w c) p", p=P)).then_inc(s_cwl, 16)
            norm_end(1, tiles(x_dram[1]))
            norm_weights(2, ln1_g[1], ln1_b[1])
            for t in range(NT):
                pool.wait_ge(s_st_x[t], 32)
            pool.wait_ge(s_tr, 32)
            residuals(2, tiles(x_dram[1]))
            norm_end(2, tiles(x_dram[2]))
            norm_weights(3, ln2_g[1], ln2_b[1])
            experts(1)
            norm_end(3, y_tiles)
            for t in range(NT):
                pool.wait_ge(s_st_x[t], 64)


_INS = ["x_prompt", "x_sample", "router_w", "router_b", "mlstm_w_in", "mlstm_b_gate", "mlstm_norm_g", "mlstm_w_out",
        "conv_w_in", "conv_w", "conv_w_out", "ln1_g", "ln1_b", "moe_w_gu", "moe_w_down", "ln2_g", "ln2_b"]


def kernel(**inputs):
    import numpy as np
    import concourse.bacc as bacc
    from concourse.bass_utils import run_bass_kernel_spmd

    nc = bacc.Bacc("TRN2", target_bir_lowering=False, num_devices=1)
    arrays, args = {}, []
    for name in _INS:
        a = np.ascontiguousarray(inputs[name])
        arrays[f"in_{name}"] = a
        args.append(nc.dram_tensor(f"in_{name}", a.shape, mybir.dt.from_np(a.dtype), kind="ExternalInput").ap())
    for name in ("x_prompt", "x_sample"):
        a = inputs[name]
        args.append(nc.dram_tensor(f"out_{name}", a.shape, F32, kind="ExternalOutput").ap())
    trunk(nc, *args)
    r = run_bass_kernel_spmd(nc, [arrays], core_ids=[0])
    return r.results[0]["out_x_prompt"], r.results[0]["out_x_sample"]
```

```python
from contextlib import ExitStack

import concourse.bass as bass
from concourse import mybir

ALU = mybir.AluOpType
ACT = mybir.ActivationFunctionType
AX = mybir.AxisListType
F32 = mybir.dt.float32
F32R = mybir.dt.float32r
I32 = mybir.dt.int32
U32 = mybir.dt.uint32

P = 128
NO_ROW = 2048.0
NEG = -1e30


class Steps:

    def __init__(self, engine, sem):
        self.engine, self.sem, self.n, self.turn = engine, sem, 0, 0

    def __call__(self, instruction):
        instruction.then_inc(self.sem, 1)
        self.n += 1

    def wait(self):
        self.engine.wait_ge(self.sem, self.turn + self.n)

    def loop(self, turn, per_turn):
        self.turn, self.before, self.per_turn = turn * per_turn, self.n, per_turn

    def end(self, turns):
        assert self.n - self.before == self.per_turn, (self.n - self.before, self.per_turn)
        self.turn, self.n = 0, self.before + turns * self.per_turn


def trunk(nc, x_prompt, x_sample, router_w, router_b, mlstm_w_in, mlstm_b_gate, mlstm_norm_g, mlstm_w_out,
          conv_w_in, conv_w, conv_w_out, ln1_g, ln1_b, moe_w_gu, moe_w_down, ln2_g, ln2_b,
          y_prompt, y_sample, PLACES=P):
    S = x_prompt.shape[1]
    D = x_prompt.shape[2]
    T = 2 * S
    NT = T // P
    KC = D // P
    E = moe_w_gu.shape[1]
    NG, GE = 4, E // 4
    FE = moe_w_down.shape[2]
    NH = mlstm_b_gate.shape[1] // 4
    HD = D // NH
    VW = HD + 2
    ALPHA = float((2.0 * 2) ** 0.25)
    LN_EPS, HEAD_EPS = 1e-5, 1e-6
    ROUNDS = -(-T // PLACES)
    UNIT = 2048
    CG = 512
    assert (S, D, NT, KC, NH, HD, FE) == (256, 1024, 4, 8, 4, 256, 256)

    MIX1_UNITS, MIX2_UNITS, MOE_UNITS = 20, 16, 3 * E
    SPLIT0 = [MIX1_UNITS, MIX1_UNITS + 2 * E + MIX2_UNITS]
    SPLIT_CONV = MIX1_UNITS + 2 * E
    HL_CREDIT = 2
    BANK_CREDIT = 8
    RING1, RINGM, RING2 = 4, 12, 6
    phases = [(RING1, MIX1_UNITS), (RINGM, MOE_UNITS), (RING2, MIX2_UNITS), (RINGM, MOE_UNITS)]
    before = []
    tally = [0] * RINGM
    for ring, units in phases:
        before.append(list(tally))
        for u in range(units):
            tally[u % ring] += 1

    ctx = ExitStack()
    with ctx:
        def sb(name, shape, dt=F32):
            return ctx.enter_context(nc.sbuf_tensor(name, shape, dt))

        def sem(name):
            return ctx.enter_context(nc.semaphore(name))

        arena = sb("arena", [P, 28704])
        xt_hi = sb("xt_hi", [P, KC, T], F32R)
        xt_lo = sb("xt_lo", [P, KC, T], F32R)
        w_hi = sb("w_hi", [P, 2, UNIT], F32R)
        w_lo = sb("w_lo", [P, 2, UNIT], F32R)
        ln_g = sb("ln_g", [P, D])
        ln_b = sb("ln_b", [P, D])
        temp = sb("temp", [P, 3072])
        ident = sb("ident", [P, P])
        pick_head = sb("pick_head", [NH, NH, P])
        mask_fw, mask_bw = ln_b[:, 0:S], ln_b[:, S:2 * S]
        earlier = sb("earlier", [P, P], F32R)
        all_ones = sb("all_ones", [P, P], F32R)
        place_no = sb("place_no", [P, P])
        gate_w_hi = sb("gate_w_hi", [P, KC, 16], F32R)
        gate_w_lo = sb("gate_w_lo", [P, KC, 16], F32R)
        rout_w_hi = sb("rout_w_hi", [P, KC, E], F32R)
        rout_w_lo = sb("rout_w_lo", [P, KC, E], F32R)
        gate_b = sb("gate_b", [16, 1])
        rout_b = sb("rout_b", [E, 1])
        eps_ln = sb("eps_ln", [P, 1])
        eps_head = sb("eps_head", [P, 1])
        taps = sb("taps", [P, 3, KC])
        cols = sb("cols", [P, 2, 2, NT, NH])
        exp_neg_m = sb("exp_neg_m", [P, 2, NT, NH])
        den = sb("den", [P, 4])
        den_rec = sb("den_rec", [P, 8, 4])
        stats = sb("stats", [P, NT, 2, 6])
        mean_var = sb("mean_var", [P, NT, 2])
        std = sb("std", [P, NT])
        rstd = sb("rstd", [P, NT])
        neg_mean_rstd = sb("neg_mean_rstd", [P, NT])
        head_stats = sb("head_stats", [P, 8, 2, 6])
        head_mv = sb("head_mv", [P, 8, 2, 2])
        head_std = sb("head_std", [P, 8, 2])
        head_rstd = sb("head_rstd", [P, 8, 2])
        token_no = sb("token_no", [P, NT])
        group_first = sb("group_first", [P, NG])
        expert_first = sb("expert_first", [P, E])
        r_one = sb("r_one", [P, NT])
        r_sum = sb("r_sum", [P, NT])
        r_v1 = sb("r_v1", [P, NT])
        r_v2 = sb("r_v2", [P, NT])
        is_top1 = sb("is_top1", [P, NT, E])
        is_top2 = sb("is_top2", [P, NT, E])
        chosen_pad = sb("chosen_pad", [P, 2 * NT + 1, E], F32R)
        chosen = chosen_pad[:, NT:2 * NT, :]
        place = sb("place", [P, NT, E])
        values = sb("values", [P, NT, E, 2], F32R)
        gate_of = sb("gate_of", [P, NT, 2])
        r_max = sb("r_max", [P, 1])
        most = sb("most", [P, 1], I32)
        rows_of = sb("rows_of", [P, E, 2], U32)

        ps = ctx.enter_context(nc.psum_tensor("ps", [P, 8, 512], F32))

        x_dram = [nc.dram_tensor(f"x_of_experts_{n}", (T, D), F32, kind="Internal").ap() for n in range(2)]
        y_dram = [nc.dram_tensor(f"expert_out_{n}", (2 * T, D), F32, kind="Internal").ap() for n in range(2)]

        def raw(slot):
            return arena[:, slot * UNIT:(slot + 1) * UNIT]

        def words(at, n):
            return arena[:, at:at + n]

        qT = words(8192, 4096).rearrange("p (c t) -> p c t", c=KC)
        kT = words(12288, 4096).rearrange("p (c t) -> p c t", c=KC)
        v_ext = words(16384, NT * NH * VW).rearrange("p (t h d) -> p t h d", t=NT, h=NH)
        o_sig = words(20512, 4096).rearrange("p (t d) -> p t d", t=NT)
        x_in = qT.rearrange("p c t -> p (c t)").rearrange("p (t d) -> p t d", t=NT)
        rest = 24608
        z = words(rest, 4096).rearrange("p (t d) -> p t d", t=NT)
        rows_i = arena[0:NH, rest:rest + 1024].rearrange("p (r t) -> p r t", r=2)
        rows_f = arena[0:NH, rest + 1024:rest + 2048].rearrange("p (r t) -> p r t", r=2)
        rows_l = arena[0:NH, rest + 2048:rest + 3072].rearrange("p (r t) -> p r t", r=2)
        rows_a = arena[0:NH, rest + 3072:rest + 4096].rearrange("p (r t) -> p r t", r=2)
        rows_c = temp[0:NH, 0:1024].rearrange("p (r t) -> p r t", r=2)
        rows_m = temp[0:NH, 1024:2048].rearrange("p (r t) -> p r t", r=2)
        exps = temp[:, 0:1536].rearrange("p (b n) -> p b n", b=2)
        probs = temp[:, 1536:3072].rearrange("p (b n) -> p b n", b=2)
        gates_T = temp[0:16, 2048:2048 + T]
        xg = words(rest, 2048).rearrange("p (b d) -> p b d", b=2)
        ye = words(rest + 2048, 2048).rearrange("p (b d) -> p b d", b=2)
        one_hot = xt_hi[:, :, 2 * P:3 * P].rearrange("p (b t) s -> p b t s", b=2)
        logits_T = temp[0:E, 0:T]
        silu_g = temp[:, 1024:1536].rearrange("p (b f) -> p b f", b=2)
        h_tok = temp[:, 1536:2048].rearrange("p (b f) -> p b f", b=2)
        h_T = temp[:, 2048:2560].rearrange("p (b k s) -> p b k s", b=2, k=2)
        gate_w = temp[:, 2560:2688].rearrange("p (k n) -> p k n", k=KC)
        rout_w = temp[:, 2688:2816].rearrange("p (k n) -> p k n", k=KC)
        r_log, r_prob, r_a, r_b = (temp[:, 2560 + 64 * n:2624 + 64 * n].rearrange("p (t e) -> p t e", t=NT)
                                   for n in range(4))
        r_pair = temp[:, 2816:2912].rearrange("p (g n) -> p g n", g=NT * NG)
        r_score, r_group = (temp[:, at:at + 16].rearrange("p (t g) -> p t g", t=NT) for at in (2912, 2928))
        conv_rows = temp[0:3 * KC, 2560:2688]
        y_back = [raw(slot).rearrange("p (k d) -> p k d", k=2) for slot in (6, 7, 8, 11)]
        x_back = words(9 * UNIT, 4096).rearrange("p (t d) -> p t d", t=NT)
        c_T = words(6 * UNIT, 2048).rearrange("p (c t) -> p c t", c=4)
        u_T = words(7 * UNIT, 2048).rearrange("p (c t) -> p c t", c=4)
        conv_T = words(8 * UNIT, 2048).rearrange("p (c t) -> p c t", c=4)
        g_T = words(9 * UNIT, 4096).rearrange("p (c t) -> p c t", c=KC)
        late_xT = words(3 * UNIT, 1024).rearrange("p (c s) -> p c s", c=KC)

        s_x = [sem(f"x_loaded{t}") for t in range(NT)]
        s_par = sem("gate_weights_loaded")
        s_rpar = sem("router_weights_loaded")
        s_cwl = sem("taps_loaded")
        s_raw = [sem(f"raw_loaded{s}") for s in range(RINGM)]
        s_const = sem("constants_made")
        s_hi = sem("unit_hi_ready")
        s_lo = sem("unit_lo_ready")
        s_hl = sem("unit_multiplied")
        s_bank = sem("bank_summed")
        s_free = sem("bank_evacuated")
        s_tr = sem("tile_half_transposed")
        s_xth = sem("xt_hi_ready")
        s_xtl = sem("xt_lo_ready")
        s_small = sem("small_split")
        s_gmm = sem("gates_multiplied")
        s_gb = sem("gates_biased")
        s_grow = sem("gates_transposed")
        s_rows = sem("gate_rows_read")
        s_soft = sem("softplus_steps")
        s_rowsd = sem("gate_rows_done")
        s_colmm = sem("columns_transposed")
        s_cols = sem("columns_read")
        s_em = sem("exp_neg_m_ready")
        s_mb = sem("maxima_spread")
        s_st = sem("scores_ready")
        s_e = sem("exponents_ready")
        s_exp = sem("exps_ready")
        s_p = sem("weights_ready")
        s_av = sem("heads_multiplied")
        s_rec = sem("denominators_ready")
        s_fwd = sem("forward_scaled")
        s_hb = sem("head_banks_read")
        s_hh = sem("heads_ready")
        s_hstd = sem("head_std_ready")
        s_og = sem("o_times_norm_ready")
        s_y = sem("mixer1_tile_ready")
        s_lnp = sem("norm_weights_loaded")
        s_res = [sem(f"residual_loaded{t}") for t in range(NT)]
        s_stat = sem("norm_stats_ready")
        s_std = sem("norm_std_ready")
        s_nmr = sem("norm_shift_ready")
        s_nrm = sem("norm_shifted")
        s_zn = sem("normalised_ready")
        s_xr = sem("x_tile_ready")
        s_xr3 = sem("x_last_tile_ready")
        s_st_x = sem("x_stored")
        s_out = sem("output_stored")
        s_xb = sem("expert_residual_loaded")
        s_yg = sem("first_result_times_gate")
        s_yx = sem("first_result_added")
        s_yb = [[sem(f"result{k}_loaded{t}") for k in range(2)] for t in range(NT)]
        s_ax = sem("residual_scaled")
        s_lg = sem("logits_multiplied")
        s_lb = sem("logits_biased")
        s_lt = sem("logits_transposed")
        s_rlog = sem("logits_shifted")
        s_rexp = sem("router_exps_ready")
        s_chosen = sem("experts_chosen")
        s_rank = sem("places_multiplied")
        s_routed = sem("routing_ready")
        s_xg0 = sem("gather_buffers_cleared")
        s_oh = sem("one_hot_ready")
        s_ixm = sem("rows_multiplied")
        s_ix = sem("row_numbers_ready")
        s_gat = [sem(f"gathered{b}") for b in range(2)]
        s_gtr = sem("gathered_transposed")
        s_ghi = sem("gathered_hi_ready")
        s_glo = sem("gathered_lo_ready")
        s_silu = sem("silu_ready")
        s_h = sem("hidden_ready")
        s_htr = sem("hidden_transposed")
        s_ht = sem("hidden_transposed_read")
        s_dn = sem("down_multiplied")
        s_ye = sem("expert_result_read")
        s_sca = [sem(f"scattered{b}") for b in range(2)]
        s_cev = sem("c_read")
        s_hev = sem("h_or_b_read")
        s_conv = sem("convolved_ready")
        s_cwt = sem("taps_transposed")
        s_taps = sem("taps_ready")
        s_ghx = sem("g_hi_ready")
        s_glx = sem("g_lo_ready")
        s_dve = sem("vector_steps")
        s_pool = sem("gpsimd_steps")
        s_act = sem("scalar_steps")
        late = [{k: sem(f"late{n}_{k}") for k in (
            "w", "free", "oh", "ixm", "ix", "gat", "tr", "xt", "gu", "silu", "h", "htr", "ht", "dn", "ye", "sca")}
            for n in range(2)]

        def raw_count(phase, u, turn=0):
            ring = phases[phase][0]
            return (turn + (before[phase][u % ring] + u // ring + 1)) * 16

        def wait_bank(eng, group, unit, c):
            if c < 3:
                eng.wait_ge(s_bank, group * 3 + (c + 1))
            else:
                eng.wait_ge(s_hl, unit + (HL_CREDIT + 1))

        def wait_x(eng, call, t):
            if t < NT - 1:
                eng.wait_ge(s_xr, (NT - 1) * call + t + 1)
            else:
                eng.wait_ge(s_xr3, call + 1)

        block = ctx.enter_context(nc.Block())

        @block.sync
        def _(sp):
            x_tiles = [x_prompt[0, 0:P, :], x_prompt[0, P:S, :], x_sample[0, 0:P, :], x_sample[0, P:S, :]]

            def rows4(w, k0, c0):
                return w[k0 * P:(k0 + 4) * P, c0:c0 + CG].rearrange("(k p) n -> p k n", p=P)

            def load(slot, src, k):
                sp.dma_start(raw(slot).rearrange("p (k n) -> p k n", k=k), src).then_inc(s_raw[slot], 16)

            w_in, w_out, cw_in, cw_out = mlstm_w_in[0], mlstm_w_out[0], conv_w_in[0], conv_w_out[0]
            for t in range(NT):
                sp.dma_start(x_in[:, t, :], x_tiles[t]).then_inc(s_x[t], 16)
                if t == 0:
                    sp.dma_start(gate_w[:, :, :], w_in[:, 4 * D:4 * D + 16].rearrange("(k p) n -> p k n", p=P)
                                 ).then_inc(s_par, 16)
                    sp.dma_start(gate_b[:, :], mlstm_b_gate.rearrange("o n -> n o")).then_inc(s_par, 16)
            u = 0
            for half in range(2):
                for part in range(4):
                    for kh in range(2):
                        if u >= RING1:
                            sp.wait_ge(s_lo, u - RING1 + 1)
                        load(u % RING1, rows4(w_in, 4 * kh, part * D + half * CG), 4)
                        if u == 3:
                            sp.dma_start(rout_w[:, :, :], router_w.rearrange("(k p) n -> p k n", p=P)
                                         ).then_inc(s_rpar, 16)
                            sp.dma_start(rout_b[:, :], router_b.rearrange("(n o) -> n o", o=1)
                                         ).then_inc(s_rpar, 16)
                        u += 1
            for half in range(2):
                for kh in range(2):
                    sp.wait_ge(s_lo, u - RING1 + 1)
                    load(u % RING1, rows4(w_out, 4 * kh, half * CG), 4)
                    u += 1

            def expert_loads(layer, turn, first):
                phase = 1 + 2 * layer
                split_phase = SPLIT0[layer]
                in_turn = [(j, k) for j in range(4) for k in range(3)]
                later = [(0, 0), (0, 1), (1, 0), (1, 1), (0, 2), (2, 0), (2, 1), (1, 2), (3, 0), (3, 1), (2, 2), (3, 2)]
                for j, k in (in_turn if first else later):
                    e = turn * 4 + j
                    u = 3 * j + k
                    if first and layer == 0:
                        if u < RING1:
                            sp.wait_ge(s_lo, MIX1_UNITS - RING1 + 1 + u)
                        else:
                            sp.wait_ge(s_tr, 16)
                    elif first:
                        if u < RING2:
                            last = max(v for v in range(MIX2_UNITS) if v % RING2 == u)
                            sp.wait_ge(s_lo, SPLIT_CONV + last + 1)
                        else:
                            sp.wait_ge(s_glx, KC)
                    elif k < 2:
                        sp.wait_ge(s_lo, turn * 8 + (split_phase - 8 + 2 * j + k + 1))
                    else:
                        sp.wait_ge(s_dn, turn * 4 + (16 * layer - 4 + j + 1))
                    if isinstance(e, int):
                        gu, dn = moe_w_gu[layer, e], moe_w_down[layer, e]
                    else:
                        gu = moe_w_gu[layer, bass.ds(e, 1)].rearrange("o r n -> (o r) n")
                        dn = moe_w_down[layer, bass.ds(e, 1)].rearrange("o r n -> (o r) n")
                    if k < 2:
                        load(u, rows4(gu, 4 * k, 0), 4)
                    else:
                        load(u, dn.rearrange("(k p) n -> p k n", p=P), 2)

            def late_loads(layer):
                L = late[layer]
                sp.wait_ge(s_routed, 1 + layer)
                n = sp.value_load(most[0:1, 0:1], min_val=0, max_val=T)
                with sp.If(n > PLACES):
                    sp.wait_ge(s_lo, SPLIT0[layer] + 2 * E)
                    sp.wait_ge(s_dn, 16 * layer + E)
                    with sp.Fori(0, E) as e:
                        sp.wait_ge(L["free"], e + 1)
                        gu = moe_w_gu[layer, bass.ds(e, 1)].rearrange("o r n -> (o r) n")
                        dn = moe_w_down[layer, bass.ds(e, 1)].rearrange("o r n -> (o r) n")
                        for k in range(2):
                            sp.dma_start(raw(k).rearrange("p (k n) -> p k n", k=4), rows4(gu, 4 * k, 0)
                                         ).then_inc(L["w"], 16)
                        sp.dma_start(raw(2).rearrange("p (k n) -> p k n", k=2),
                                     dn.rearrange("(k p) n -> p k n", p=P)).then_inc(L["w"], 16)
                    sp.wait_ge(L["free"], E + 1)
                    sp.wait_ge(L["sca"], 16 * E * (ROUNDS - 1))

            def tiles(a):
                return [a[t * P:(t + 1) * P, :] for t in range(NT)]

            def stores(call, targets, sem):
                for t in range(NT):
                    wait_x(sp, call, t)
                    sp.dma_start(targets[t], z[:, t, :]).then_inc(sem, 16)

            def come_back(layer):
                sp.wait_ge(s_st_x, 64 * (layer + 1))
                sp.wait_ge(s_lo, SPLIT0[layer] + 2 * E)
                sp.dma_start(x_back, x_dram[layer].rearrange("(t p) d -> p t d", p=P)).then_inc(s_xb, 16)
                for b in range(2):
                    sp.wait_ge(s_sca[b], 16 * (E // 2) * (layer + 1))
                for t in range(NT):
                    for k in range(2):
                        row = k * T + t * P
                        sp.dma_start(y_back[t][:, k, :], y_dram[layer][row:row + P, :]).then_inc(s_yb[t][k], 16)

            expert_loads(0, 0, True)
            stores(0, tiles(x_dram[0]), s_st_x)
            with sp.Fori(1, 4) as turn:
                expert_loads(0, turn, False)
            late_loads(0)
            come_back(0)
            u = 0
            order = [(cw_in, part * D + half * CG) for half in range(2) for part in (1, 2, 0)]
            order += [(cw_out, half * CG) for half in range(2)]
            for w, c0 in order:
                for kh in range(2):
                    if u < RING2:
                        if u % 3 < 2:
                            sp.wait_ge(s_lo, SPLIT0[0] + 2 * (12 + u // 3) + u % 3 + 1)
                        else:
                            sp.wait_ge(s_dn, 12 + u // 3 + 1)
                    else:
                        sp.wait_ge(s_lo, SPLIT_CONV + u - RING2 + 1)
                    load(u % RING2, rows4(w, 4 * kh, c0), 4)
                    u += 1
            expert_loads(1, 0, True)
            stores(2, tiles(x_dram[1]), s_st_x)
            with sp.Fori(1, 4) as turn:
                expert_loads(1, turn, False)
            late_loads(1)
            come_back(1)
            stores(3, [y_prompt[0, 0:P, :], y_prompt[0, P:S, :], y_sample[0, 0:P, :], y_sample[0, P:S, :]], s_out)
            sp.wait_ge(s_out, 64)

        @block.tensor
        def _(pe):
            def products(out, pairs, first, last):
                for n, (a, b) in enumerate(pairs):
                    ins = pe.matmul(out, a, b, start=first and n == 0, stop=last and n == 2)
                return ins

            def transpose_halves(stage, source, ready):
                for t in range(NT):
                    ready(t)
                    for half in range(2):
                        if stage == 1 and half == 1:
                            pe.wait_ge(s_hb, 8)
                        for c in range(4):
                            f0 = (4 * half + c) * P
                            ins = pe.transpose(ps[:, 4 * half + t, c * P:(c + 1) * P],
                                               source[:, t, f0:f0 + P], ident[:, :])
                        ins.then_inc(s_tr, 1)

            def unit_features(s, kh, bank0, before_bank, count):
                for c in range(4):
                    before_bank(c)
                    for k in range(4):
                        w = slice(k * CG + c * P, k * CG + (c + 1) * P)
                        x = 4 * kh + k
                        ins = products(ps[:, bank0 + c, :],
                                       [(w_hi[:, s, w], xt_hi[:, x, :]), (w_hi[:, s, w], xt_lo[:, x, :]),
                                        (w_lo[:, s, w], xt_hi[:, x, :])],
                                       kh == 0 and k == 0, kh == 1 and k == 3)
                    if c == 3:
                        ins.then_inc(s_hl, 1)
                    elif count:
                        ins.then_inc(s_bank, 1)

            def unit_tokens(s, kh, bank0, before_bank, count):
                for t in range(NT):
                    before_bank(t)
                    tok = slice(t * P, (t + 1) * P)
                    for k in range(4):
                        w = slice(k * CG, (k + 1) * CG)
                        x = 4 * kh + k
                        ins = products(ps[:, bank0 + t, :],
                                       [(xt_hi[:, x, tok], w_hi[:, s, w]), (xt_hi[:, x, tok], w_lo[:, s, w]),
                                        (xt_lo[:, x, tok], w_hi[:, s, w])],
                                       kh == 0 and k == 0, kh == 1 and k == 3)
                    if t == 3:
                        ins.then_inc(s_hl, 1)
                    elif count:
                        ins.then_inc(s_bank, 1)

            def small_times(w_h, w_l, tok):
                for k in range(KC):
                    ins = products(ps[0:16, 0, tok],
                                   [(w_h[:, k, :], xt_hi[:, k, tok]), (w_h[:, k, :], xt_lo[:, k, tok]),
                                    (w_l[:, k, :], xt_hi[:, k, tok])], k == 0, k == KC - 1)
                return ins

            nothing = lambda c: None
            pe.wait_ge(s_const, 1)
            transpose_halves(0, x_in, lambda t: pe.wait_ge(s_x[t], 16))
            pe.wait_ge(s_small, 2)
            pe.wait_ge(s_xtl, 8)
            small_times(gate_w_hi, gate_w_lo, slice(0, T)).then_inc(s_gmm, 1)
            pe.wait_ge(s_gb, 1)
            for kind in range(4):
                ins = pe.matmul(ps[0:NH, 4 + kind, :], ident[0:16, kind * NH:(kind + 1) * NH], gates_T,
                                start=True, stop=True)
            ins.then_inc(s_grow, 1)
            with pe.Fori(0, 2) as half:
                for g in range(4):
                    for kh in range(2):
                        pe.wait_ge(s_lo, half * 8 + (2 * g + kh + 1))
                        if kh == 0 and g == 1:
                            pe.wait_ge(s_rows, 1)
                        if kh == 0:
                            wait = lambda c, g=g: pe.wait_ge(s_free, half * 16 + (4 * g + c + 1))
                        else:
                            wait = nothing
                        (unit_features if g < 2 else unit_tokens)(kh, kh, 4 * (g % 2), wait, kh == 1)

            pe.wait_ge(s_rowsd, 1)
            pe.wait_ge(s_free, BANK_CREDIT + 32)
            for q, rows in enumerate((rows_a, rows_i)):
                for r in range(2):
                    for t in range(NT):
                        at = ((q * 2 + r) * NT + t) * NH
                        ins = pe.transpose(ps[:, 7, at:at + NH], rows[:, r, t * P:(t + 1) * P], ident[0:NH, 0:NH])
            ins.then_inc(s_colmm, 1)

            def head_maxima(hb):
                b, h = divmod(hb, NH)
                tok = slice(b * S, (b + 1) * S)
                if hb >= 2:
                    pe.wait_ge(s_e, hb - 1)
                for r in range(2):
                    ins = pe.matmul(ps[:, 2 + hb % 2, r * S:(r + 1) * S], pick_head[:, h, :], rows_l[:, r, tok],
                                    start=True, stop=True)
                ins.then_inc(s_mb, 1)

            def head_scores(hb):
                b, h = divmod(hb, NH)
                tok = slice(b * S, (b + 1) * S)
                if hb >= 2:
                    pe.wait_ge(s_p, hb - 1)
                for j in range(2):
                    for dc in range(2):
                        ins = pe.matmul(ps[:, hb % 2, j * S:(j + 1) * S],
                                        kT[:, 2 * h + dc, b * S + j * P:b * S + (j + 1) * P],
                                        qT[:, 2 * h + dc, tok], start=dc == 0, stop=dc == 1)
                ins.then_inc(s_st, 1)

            def head_values(hb):
                b, h = divmod(hb, NH)
                p = probs[:, hb % 2, :]
                pe.wait_ge(s_p, hb + 1)
                if hb:
                    pe.wait_ge(s_hb, hb)
                else:
                    pe.wait_ge(s_cols, 1)
                sums = [[(p[:, 0:128], 0)], [(p[:, 128:256], 0), (p[:, 256:384], 1)],
                        [(p[:, 384:512], 0), (p[:, 512:640], 1)], [(p[:, 640:768], 1)]]
                for n, terms in enumerate(sums):
                    for m, (w, j) in enumerate(terms):
                        ins = pe.matmul(ps[:, 4 + n, 0:HD + 1], w, v_ext[:, 2 * b + j, h, 0:HD + 1],
                                        start=m == 0, stop=m == len(terms) - 1)
                ins.then_inc(s_av, 1)

            pe.wait_ge(s_const, 2)
            head_maxima(0)
            head_maxima(1)
            head_scores(0)
            for hb in range(8):
                if hb < 6:
                    head_maxima(hb + 2)
                if hb < 7:
                    head_scores(hb + 1)
                head_values(hb)

            def out_projection(first_unit, first_bank, chunks_ready=0):
                for half in range(2):
                    for kh in range(2):
                        n = first_unit + 2 * half + kh
                        if half == 0 and chunks_ready:
                            pe.wait_ge(s_glx, 4 * (kh + 1))
                        pe.wait_ge(s_lo, n + 1)
                        unit_tokens(kh, kh, 4 * half, first_bank if n == first_unit else nothing, kh == 1)

            transpose_halves(1, o_sig, lambda t: pe.wait_ge(s_y, t + 1))
            out_projection(16, lambda t: pe.wait_ge(s_xtl, 8 + 2 * t + 2))

            def router_half(layer, half):
                pe.wait_ge(s_small, 4)
                pe.wait_ge(s_xtl, 8 * (2 + 2 * layer) + 4 * half + 4)
                return small_times(rout_w_hi, rout_w_lo, slice(half * S, (half + 1) * S))

            def router(layer):
                router_half(layer, 0)
                router_half(layer, 1).then_inc(s_lg, 1)
                pe.wait_ge(s_lb, layer + 1)
                for t in range(NT):
                    ins = pe.transpose(ps[:, 2, t * E:(t + 1) * E], logits_T[:, t * P:(t + 1) * P],
                                       ident[0:E, 0:E])
                ins.then_inc(s_lt, 1)
                pe.wait_ge(s_chosen, layer + 1)
                out = ps[:, 1, 0:(NT + 1) * E]
                pe.matmul(out, earlier[:, :], slots(NT), start=True, stop=False)
                for back in range(1, NT + 1):
                    ins = pe.matmul(out, all_ones[:, :], slots(NT - back), start=False, stop=back == NT)
                ins.then_inc(s_rank, 1)

            def slots(first):
                return chosen_pad[:, first:first + NT + 1, :].rearrange("p s e -> p (s e)")

            def experts(layer):
                c0 = E * layer

                def rows_mm(e, j):
                    pe.wait_ge(s_oh, e + (c0 + 1))
                    if not isinstance(e, int) or e >= 1:
                        pe.wait_ge(s_ix, e + c0)
                    for t in range(NT):
                        rhs = values[:, t, e, :] if isinstance(e, int) else \
                            values[:, t, bass.ds(e, 1), :].rearrange("p o n -> p (o n)")
                        ins = pe.matmul(ps[:, 7, 0:2], one_hot[:, j % 2, t, :], rhs,
                                        start=t == 0, stop=t == NT - 1)
                    ins.then_inc(s_ixm, 1)

                def tokens_T(e, j):
                    pe.wait_ge(s_gat[j % 2], 16 * ((E // 2) * layer) + gathers(e, j))
                    if not isinstance(e, int) or e >= 1:
                        pe.wait_ge(s_glo, e + c0)
                    for c in range(KC):
                        ins = pe.transpose(ps[:, c // 4, (c % 4) * P:(c % 4 + 1) * P],
                                           xg[:, j % 2, c * P:(c + 1) * P], ident[:, :])
                    ins.then_inc(s_gtr, 1)

                def gate_up(e, j):
                    pe.wait_ge(s_glo, e + (c0 + 1))
                    if not isinstance(e, int) or e >= 2:
                        pe.wait_ge(s_h, e + (c0 - 1))
                    for kh in range(2):
                        pe.wait_ge(s_lo, e * 2 + (SPLIT0[layer] + kh + 1))
                        tok = slice((j % 2) * P, (j % 2 + 1) * P)
                        for k in range(4):
                            w = slice(k * CG, (k + 1) * CG)
                            x = 4 * kh + k
                            ins = products(ps[:, 2 + j % 2, :],
                                           [(xt_hi[:, x, tok], w_hi[:, kh, w]), (xt_hi[:, x, tok], w_lo[:, kh, w]),
                                            (xt_lo[:, x, tok], w_hi[:, kh, w])],
                                           kh == 0 and k == 0, kh == 1 and k == 3)
                        ins.then_inc(s_hl, 1)

                def hidden_T(e, j):
                    pe.wait_ge(s_h, e + (c0 + 1))
                    if not isinstance(e, int) or e >= 1:
                        pe.wait_ge(s_ht, e + c0)
                    for k in range(2):
                        ins = pe.transpose(ps[:, 4, k * P:(k + 1) * P], h_tok[:, j % 2, k * P:(k + 1) * P],
                                           ident[:, :])
                    ins.then_inc(s_htr, 1)

                def down(e, j, turn):
                    pe.wait_ge(s_ht, e + (c0 + 1))
                    pe.wait_ge(s_raw[3 * j + 2], raw_count(1 + 2 * layer, 3 * j + 2, turn))
                    if not isinstance(e, int) or e >= 1:
                        pe.wait_ge(s_ye, e + c0)
                    for half in range(2):
                        for k in range(2):
                            ins = pe.matmul(ps[:, 5 + half, :], h_T[:, j % 2, k, :],
                                            raw(3 * j + 2)[:, k * D + half * CG:k * D + (half + 1) * CG],
                                            start=k == 0, stop=k == 1)
                    ins.then_inc(s_dn, 1)

                def gathers(e, j):
                    return (e - (j % 2)) * 8 + 16

                def step(e, j, turn, left):
                    hidden_T(e, j)
                    if left > 2:
                        tokens_T(e + 2, (j + 2) % 4)
                    if left > 1:
                        gate_up(e + 1, (j + 1) % 4)
                    if left > 4:
                        rows_mm(e + 4, j)
                    down(e, j, turn)

                for e in range(3):
                    rows_mm(e, e)
                pe.wait_ge(s_routed, layer + 1)
                tokens_T(0, 0)
                rows_mm(3, 3)
                tokens_T(1, 1)
                gate_up(0, 0)
                with pe.Fori(0, 3) as turn:
                    for j in range(4):
                        step(turn * 4 + j, j, turn, 9)
                for j in range(4):
                    step(12 + j, j, 3, 4 - j)

            def late_experts(layer):
                L = late[layer]
                n = pe.value_load(most[0:1, 0:1], min_val=0, max_val=T)
                with pe.If(n > PLACES):
                    pe.wait_ge(s_ye, E * layer + E)
                    pe.nop().then_inc(L["free"], 1)
                    with pe.Fori(0, E) as e:
                        pe.wait_ge(L["w"], e * 48 + 48)
                        for r in range(1, ROUNDS):
                            n = e * (ROUNDS - 1) + r
                            pe.wait_ge(L["oh"], n)
                            for t in range(NT):
                                ins = pe.matmul(ps[:, 7, 0:2], one_hot[:, 0, t, :],
                                                values[:, t, bass.ds(e, 1), :].rearrange("p o n -> p (o n)"),
                                                start=t == 0, stop=t == NT - 1)
                            ins.then_inc(L["ixm"], 1)
                            pe.wait_ge(L["gat"], n * 16)
                            for c in range(KC):
                                ins = pe.transpose(ps[:, c // 4, (c % 4) * P:(c % 4 + 1) * P],
                                                   xg[:, 0, c * P:(c + 1) * P], ident[:, :])
                            ins.then_inc(L["tr"], 1)
                            pe.wait_ge(L["xt"], n)
                            for k in range(KC):
                                ins = pe.matmul(ps[:, 2, :], late_xT[:, k, :],
                                                raw(k // 4)[:, (k % 4) * CG:(k % 4 + 1) * CG],
                                                start=k == 0, stop=k == KC - 1)
                            ins.then_inc(L["gu"], 1)
                            pe.wait_ge(L["h"], n)
                            for k in range(2):
                                ins = pe.transpose(ps[:, 4, k * P:(k + 1) * P], h_tok[:, 0, k * P:(k + 1) * P],
                                                   ident[:, :])
                            ins.then_inc(L["htr"], 1)
                            pe.wait_ge(L["ht"], n)
                            for half in range(2):
                                for k in range(2):
                                    ins = pe.matmul(ps[:, 5 + half, :], h_T[:, 0, k, :],
                                                    raw(2)[:, k * D + half * CG:k * D + (half + 1) * CG],
                                                    start=k == 0, stop=k == 1)
                            ins.then_inc(L["dn"], 1)
                            pe.wait_ge(L["ye"], n)
                        pe.nop().then_inc(L["free"], 1)

            transpose_halves(2, z, lambda t: wait_x(pe, 0, t))
            router(0)
            experts(0)
            late_experts(0)
            transpose_halves(3, z, lambda t: wait_x(pe, 1, t))
            pe.wait_ge(s_cwl, 16)
            pe.wait_ge(s_xtl, 32)
            pe.transpose(ps[:, 7, 0:3 * KC], conv_rows[:, :], ident[0:3 * KC, 0:3 * KC]).then_inc(s_cwt, 1)
            pe.wait_ge(s_taps, 1)
            with pe.Fori(0, 2) as half:
                for g in range(3):
                    for kh in range(2):
                        pe.wait_ge(s_lo, half * 6 + (SPLIT_CONV + 2 * g + kh + 1))
                        wait = nothing
                        if kh == 0 and g == 0:
                            wait = lambda c: pe.wait_ge(s_hev, half * 8 + (c + 1))
                        if kh == 0 and g == 2:
                            wait = lambda c: pe.wait_ge(s_cev, half * 4 + (c + 1))
                        unit_features(kh, kh, 4 * (g % 2), wait, kh == 1)
            out_projection(SPLIT_CONV + 12, nothing, KC)
            transpose_halves(4, z, lambda t: wait_x(pe, 2, t))
            router(1)
            experts(1)
            late_experts(1)

        @block.scalar
        def _(act):
            def unit_hi(n, slot, loaded, parity):
                act.wait_ge(s_raw[slot], loaded)
                act.wait_ge(s_hl, n + 1)
                act.activation(w_hi[:, parity, :], raw(slot), ACT.Copy).then_inc(s_hi, 1)

            def halves_hi(stage, tiles=range(NT)):
                for t in tiles:
                    for half in range(2):
                        act.wait_ge(s_tr, 8 * stage + 2 * t + half + 1)
                        act.activation(xt_hi[:, 4 * half:4 * half + 4, t * P:(t + 1) * P],
                                       ps[:, 4 * half + t, :].rearrange("p (c s) -> p c s", c=4),
                                       ACT.Copy).then_inc(s_xth, 1)

            def norm_std(call, stage):
                def root(t):
                    act.wait_ge(s_stat, 4 * call + t + 1)
                    act.activation(std[:, t:t + 1], mean_var[:, t, 1:2], ACT.Sqrt, bias=eps_ln[:, :]
                                   ).then_inc(s_std, 1)

                def shift(t):
                    act.wait_ge(s_nmr, 4 * call + t + 1)
                    act.activation(z[:, t, :], z[:, t, :], ACT.Identity, bias=neg_mean_rstd[:, t:t + 1],
                                   scale=rstd[:, t:t + 1]).then_inc(s_nrm, 1)

                def first_result(t):
                    if call % 2:
                        act.wait_ge(s_yb[t][0], 16 * (call // 2 + 1))
                        act.activation(y_back[t][:, 0, :], y_back[t][:, 0, :], ACT.Copy,
                                       scale=gate_of[:, t, 0:1]).then_inc(s_yg, 1)

                root(0)
                first_result(2)
                root(1)
                first_result(3)
                shift(0)
                root(2)
                shift(1)
                root(3)
                shift(2)
                shift(3)
                if stage:
                    halves_hi(stage)

            halves_hi(0)
            act.wait_ge(s_par, 32)
            act.activation(gate_w_hi[:, :, :], gate_w[:, :, :], ACT.Copy).then_inc(s_act, 1)
            for u in range(2):
                unit_hi(u, u, raw_count(0, u), u)
            act.wait_ge(s_soft, 1)
            act.activation(rows_l, rows_l, ACT.Exp).then_inc(s_soft, 1)
            act.wait_ge(s_soft, 2)
            act.activation(rows_l, rows_l, ACT.Ln, bias=1.0).then_inc(s_soft, 1)
            act.wait_ge(s_rpar, 32)
            act.activation(rout_w_hi[:, :, :], rout_w[:, :, :], ACT.Copy).then_inc(s_act, 1)
            with act.Fori(0, 2) as half:
                for g in range(4):
                    for kh in range(2 if g < 3 else 1):
                        u = 2 * g + kh + 2
                        unit_hi(half * 8 + u, u % RING1, raw_count(0, u, half * 2), kh)
                    for c in range(4):
                        wait_bank(act, half * 4 + g, half * 8 + (2 * g + 1), c)
                        bank = ps[:, 4 * (g % 2) + c, :]
                        if g == 0:
                            dst = qT[:, bass.ds(half * 4 + c, 1), :].rearrange("p o t -> p (o t)")
                            act.activation(dst, bank, ACT.Copy).then_inc(s_free, 1)
                        elif g == 1:
                            dst = kT[:, bass.ds(half * 4 + c, 1), :].rearrange("p o t -> p (o t)")
                            act.activation(dst, bank, ACT.Copy, scale=HD ** -0.5).then_inc(s_free, 1)
                        elif g == 2:
                            act.activation(v_ext[:, c, bass.ds(half * 2, 2), 0:HD],
                                           bank.rearrange("p (h d) -> p h d", h=2), ACT.Copy).then_inc(s_free, 1)
                        else:
                            act.activation(o_sig[:, c, bass.ds(half * CG, CG)], bank, ACT.Sigmoid
                                           ).then_inc(s_free, 1)
                unit_hi(half * 8 + 9, 9 % RING1, raw_count(0, 9, half * 2), 1)
            act.wait_ge(s_cols, 1)
            act.activation(exp_neg_m[:, :, :, :], cols[:, 1], ACT.Exp, scale=-1.0).then_inc(s_em, 1)

            def head_exp(hb):
                act.wait_ge(s_e, hb + 1)
                act.activation(exps[:, hb % 2, :], exps[:, hb % 2, :], ACT.Exp).then_inc(s_exp, 1)

            def forward_scale(hb):
                b, h = divmod(hb, NH)
                act.wait_ge(s_rec, hb + 1)
                for it in range(2):
                    act.activation(qT[:, 2 * h + it, b * S:(b + 1) * S], ps[:, 4 + it, 0:HD], ACT.Copy,
                                   scale=den_rec[:, hb, it:it + 1]).then_inc(s_fwd, 1)

            act.wait_ge(s_const, 2)
            head_exp(0)
            head_exp(1)
            for hb in range(8):
                if hb < 6:
                    head_exp(hb + 2)
                forward_scale(hb)
                if hb == 3 or hb == 7:
                    act.wait_ge(s_hh, hb + 1)
                    act.activation(head_std[:, hb - 3:hb + 1, :], head_mv[:, hb - 3:hb + 1, :, 1], ACT.Sqrt,
                                   bias=eps_head[:, :]).then_inc(s_hstd, 1)
            halves_hi(1)
            for n in (18, 19):
                unit_hi(n, n % RING1, raw_count(0, n), n % 2)
            norm_std(0, 2)

            def router_exp(layer):
                for kh in range(2):
                    unit_hi(SPLIT0[layer] + kh, kh, raw_count(1 + 2 * layer, kh), kh)
                for t in range(NT):
                    act.wait_ge(s_rlog, NT * layer + t + 1)
                    act.activation(r_prob[:, t, :], r_log[:, t, :], ACT.Exp, accum_out=r_sum[:, t:t + 1]
                                   ).then_inc(s_rexp, 1)

            def experts(layer):
                c0 = E * layer

                def gathered_hi(e, j):
                    act.wait_ge(s_gtr, e + (c0 + 1))
                    act.activation(xt_hi[:, :, (j % 2) * P:(j % 2 + 1) * P],
                                   ps[:, 0:2, :].rearrange("p b (c s) -> p (b c) s", c=4), ACT.Copy
                                   ).then_inc(s_ghi, 1)

                def silu(e, j):
                    act.wait_ge(s_hl, e * 2 + (SPLIT0[layer] + 2 + HL_CREDIT))
                    act.activation(silu_g[:, j % 2, :], ps[:, 2 + j % 2, 0:FE], ACT.Silu).then_inc(s_silu, 1)

                def hidden_read(e, j):
                    act.wait_ge(s_htr, e + (c0 + 1))
                    act.activation(h_T[:, j % 2].rearrange("p k s -> p (k s)"), ps[:, 4, 0:2 * P], ACT.Copy
                                   ).then_inc(s_ht, 1)

                def result_read(e, j):
                    act.wait_ge(s_dn, e + (c0 + 1))
                    if not isinstance(e, int) or e >= 2:
                        act.wait_ge(s_sca[j % 2], (e - (j % 2)) * 8 + 16 * (E // 2) * layer)
                    act.activation(ye[:, j % 2, :], ps[:, 5:7, :].rearrange("p b n -> p (b n)"), ACT.Copy
                                   ).then_inc(s_ye, 1)

                def units(e, j, turn, kh):
                    unit_hi(e * 2 + (SPLIT0[layer] + kh), 3 * j + kh, raw_count(1 + 2 * layer, 3 * j + kh, turn), kh)

                def step(e, j, turn, left):
                    hidden_read(e, j)
                    if left > 2:
                        gathered_hi(e + 2, (j + 2) % 4)
                        units(e + 2, (j + 2) % 4, turn + (1 if j >= 2 else 0), 0)
                    if left > 1:
                        silu(e + 1, (j + 1) % 4)
                    if left > 2:
                        units(e + 2, (j + 2) % 4, turn + (1 if j >= 2 else 0), 1)
                    result_read(e, j)

                gathered_hi(0, 0)
                gathered_hi(1, 1)
                units(1, 1, 0, 0)
                silu(0, 0)
                units(1, 1, 0, 1)
                for j in range(4):
                    step(j, j, 0, 9)
                with act.Fori(1, 3) as turn:
                    for j in range(4):
                        step(turn * 4 + j, j, turn, 9)
                for j in range(4):
                    step(12 + j, j, 3, 4 - j)

            def late_experts(layer):
                L = late[layer]
                n = act.value_load(most[0:1, 0:1], min_val=0, max_val=T)
                with act.If(n > PLACES):
                    act.wait_ge(s_sca[0], 16 * (E // 2) * (layer + 1))
                    with act.Fori(0, E) as e:
                        for r in range(1, ROUNDS):
                            n = e * (ROUNDS - 1) + r
                            act.wait_ge(L["tr"], n)
                            act.activation(late_xT.rearrange("p c s -> p (c s)"),
                                           ps[:, 0:2, :].rearrange("p b n -> p (b n)"), ACT.Copy).then_inc(L["xt"], 1)
                            act.wait_ge(L["gu"], n)
                            act.activation(silu_g[:, 0, :], ps[:, 2, 0:FE], ACT.Silu).then_inc(L["silu"], 1)
                            act.wait_ge(L["htr"], n)
                            act.activation(h_T[:, 0].rearrange("p k s -> p (k s)"), ps[:, 4, 0:2 * P], ACT.Copy
                                           ).then_inc(L["ht"], 1)
                            act.wait_ge(L["dn"], n)
                            act.activation(ye[:, 0, :], ps[:, 5:7, :].rearrange("p b n -> p (b n)"), ACT.Copy
                                           ).then_inc(L["ye"], 1)
                            act.wait_ge(L["sca"], n * 16)

            def scale_residual(call):
                act.wait_ge(s_xb, 16 * (call // 2 + 1))
                for t in range(NT):
                    act.activation(x_back[:, t, :], x_back[:, t, :], ACT.Copy, scale=ALPHA).then_inc(s_ax, 1)

            router_exp(0)
            experts(0)
            late_experts(0)
            scale_residual(1)
            norm_std(1, 3)
            unit_hi(SPLIT_CONV, 0, raw_count(2, 0), 0)
            with act.Fori(0, 2) as half:
                unit_hi(half * 6 + (SPLIT_CONV + 1), 1, raw_count(2, 1, half), 1)
                for g in range(3):
                    for kh in range(2):
                        u = 2 * g + kh + 2
                        if u < 7:
                            unit_hi(half * 6 + (SPLIT_CONV + u), u % RING2, raw_count(2, u, half), kh)
                    if g == 0:
                        for c in range(4):
                            wait_bank(act, half * 3 + 10, half * 6 + (SPLIT_CONV + 1), c)
                            act.activation(c_T[:, c, :], ps[:, c, :], ACT.Copy).then_inc(s_cev, 1)
            for c in range(KC):
                act.wait_ge(s_conv, 4 * (c // 4 + 1))
                act.wait_ge(s_hl, SPLIT_CONV + 12 + HL_CREDIT)
                act.activation(xt_hi[:, c, :], g_T[:, c, :], ACT.Copy).then_inc(s_ghx, 1)
            unit_hi(SPLIT_CONV + 13, 13 % RING2, raw_count(2, 13), 1)
            for n in (14, 15):
                unit_hi(SPLIT_CONV + n, n % RING2, raw_count(2, n), n % 2)
            norm_std(2, 4)
            router_exp(1)
            experts(1)
            late_experts(1)
            scale_residual(3)
            norm_std(3, 0)

        @block.vector
        def _(dve):
            step_done = Steps(dve, s_dve)

            def do(ins):
                step_done(ins)
                step_done.wait()

            def unit_lo(n, slot, parity):
                dve.wait_ge(s_hi, n + 1)
                dve.tensor_tensor(w_lo[:, parity, :], raw(slot), w_hi[:, parity, :].bitcast(F32), ALU.subtract
                                  ).then_inc(s_lo, 1)

            def half_lo(stage, t):
                for half in range(2):
                    dve.wait_ge(s_xth, 8 * stage + 2 * t + half + 1)
                    hb = xt_hi[:, 4 * half:4 * half + 4, t * P:(t + 1) * P]
                    dve.tensor_tensor(xt_lo[:, 4 * half:4 * half + 4, t * P:(t + 1) * P],
                                      ps[:, 4 * half + t, :].rearrange("p (c s) -> p c s", c=4),
                                      hb.bitcast(F32), ALU.subtract).then_inc(s_xtl, 1)

            def norm(call, stage, sum_tile):
                def stat(t):
                    sum_tile(t)
                    for hf in range(2):
                        step_done(dve.bn_stats(stats[:, t, hf, :], z[:, t, hf * CG:(hf + 1) * CG]))
                    step_done.wait()
                    dve.bn_aggr(mean_var[:, t, :], stats[:, t, :, :].rearrange("p a b -> p (a b)")
                                ).then_inc(s_stat, 1)

                def shift_and_scale(t):
                    dve.wait_ge(s_std, 4 * call + t + 1)
                    do(dve.reciprocal(rstd[:, t:t + 1], std[:, t:t + 1]))
                    dve.tensor_scalar(neg_mean_rstd[:, t:t + 1], mean_var[:, t, 0:1], rstd[:, t:t + 1], -1.0,
                                      ALU.mult, ALU.mult).then_inc(s_nmr, 1)

                def times_g(t):
                    dve.wait_ge(s_nrm, 4 * call + t + 1)
                    if t == 0:
                        dve.wait_ge(s_lnp, 16 + 32 * (call + 1))
                    if t < NT - 1:
                        dve.tensor_tensor(z[:, t, :], z[:, t, :], ln_g[:, :], ALU.mult).then_inc(s_zn, 1)
                    else:
                        do(dve.tensor_tensor(z[:, t, :], z[:, t, :], ln_g[:, :], ALU.mult))
                        dve.tensor_tensor(z[:, t, :], z[:, t, :], ln_b[:, :], ALU.add).then_inc(s_xr3, 1)

                stat(0)
                stat(1)
                shift_and_scale(0)
                stat(2)
                shift_and_scale(1)
                times_g(0)
                stat(3)
                shift_and_scale(2)
                times_g(1)
                shift_and_scale(3)
                times_g(2)
                times_g(3)
                if stage:
                    for t in range(NT):
                        half_lo(stage, t)

            dve.engine_nop().then_inc(s_hl, HL_CREDIT)
            dve.engine_nop().then_inc(s_free, BANK_CREDIT)
            dve.engine_nop().then_inc(s_hev, 4)
            dve.memset(v_ext[:, :, :, HD:VW], 1.0).then_inc(s_dve, 1)
            step_done.n += 1
            for t in range(NT):
                half_lo(0, t)
            dve.wait_ge(s_act, 1)
            dve.tensor_tensor(gate_w_lo[:, :, :], gate_w[:, :, :], gate_w_hi[:, :, :].bitcast(F32), ALU.subtract
                              ).then_inc(s_small, 2)
            for u in range(2):
                unit_lo(u, u, u)
            dve.wait_ge(s_gmm, 1)
            dve.tensor_scalar(gates_T, ps[0:16, 0, :], gate_b[:, :], None, ALU.add).then_inc(s_gb, 1)
            dve.wait_ge(s_grow, 1)
            do(dve.tensor_copy(rows_f, ps[0:NH, 5:8:2, :]))
            dve.tensor_copy(rows_i, ps[0:NH, 4:7:2, :]).then_inc(s_rows, 1)
            dve.scalar_tensor_tensor(out=rows_l, in0=rows_f, scalar=-1.0, in1=rows_f, op0=ALU.mult, op1=ALU.min
                                     ).then_inc(s_soft, 1)
            dve.wait_ge(s_soft, 3)
            do(dve.scalar_tensor_tensor(out=rows_f, in0=rows_f, scalar=0.0, in1=rows_l, op0=ALU.min,
                                        op1=ALU.subtract))
            def along(rows, r, b):
                part = rows[:, r, b * S:(b + 1) * S]
                return part[:, ::-1] if r else part
            for r in range(2):
                for b in range(2):
                    step_done(dve.tensor_tensor_scan(along(rows_c, r, b), along(rows_f, r, b), along(rows_f, r, b),
                                                     0.0, ALU.add, ALU.bypass))
            step_done.wait()
            dve.wait_ge(s_rows, 1)
            do(dve.tensor_tensor(rows_a, rows_i, rows_c, ALU.subtract))
            for r in range(2):
                for b in range(2):
                    step_done(dve.tensor_tensor_scan(along(rows_m, r, b), along(rows_a, r, b), along(rows_a, r, b),
                                                     NEG, ALU.max, ALU.bypass))
            step_done.wait()
            do(dve.tensor_tensor(rows_i, rows_c, rows_m, ALU.add))
            dve.tensor_scalar(rows_l, rows_m, -1.0, None, ALU.mult).then_inc(s_rowsd, 1)
            dve.wait_ge(s_act, 2)
            dve.tensor_tensor(rout_w_lo[:, :, :], rout_w[:, :, :], rout_w_hi[:, :, :].bitcast(F32), ALU.subtract
                              ).then_inc(s_small, 2)
            with dve.Fori(0, 2) as half:
                for g in range(4):
                    for kh in range(2):
                        u = 2 * g + kh + 2
                        unit_lo(half * 8 + u, u % RING1, kh)
            dve.wait_ge(s_colmm, 1)
            dve.tensor_copy(cols[:, :, :, :, :].rearrange("p a r t h -> p (a r t h)"), ps[:, 7, 0:64]
                            ).then_inc(s_cols, 1)
            dve.wait_ge(s_cols, 1)

            def head_exponents(hb):
                b, h = divmod(hb, NH)
                dve.wait_ge(s_mb, hb + 1)
                if hb >= 2:
                    dve.wait_ge(s_p, hb - 1)
                else:
                    dve.wait_ge(s_rowsd, 1)
                x, m = exps[:, hb % 2, :], ps[:, 2 + hb % 2, :]
                a = lambda r, j: cols[:, 0, r, 2 * b + j, h:h + 1]
                for out, spread, col, mask in (
                        (x[:, 0:256], m[:, 0:256], a(0, 0), mask_fw[:, 0:256]),
                        (x[:, 256:384], m[:, 128:256], a(0, 1), mask_fw[:, 0:128]),
                        (x[:, 384:512], m[:, 256:384], a(1, 0), mask_bw[:, 128:256]),
                        (x[:, 512:768], m[:, 256:512], a(1, 1), mask_bw[:, 0:256])):
                    ins = dve.scalar_tensor_tensor(out=out, in0=spread, scalar=col, in1=mask, op0=ALU.add,
                                                   op1=ALU.min)
                ins.then_inc(s_e, 1)

            def head_weights(hb):
                dve.wait_ge(s_exp, hb + 1)
                dve.wait_ge(s_st, hb + 1)
                if hb >= 2:
                    dve.wait_ge(s_av, hb - 1)
                x, w, s = exps[:, hb % 2, :], probs[:, hb % 2, :], ps[:, hb % 2, :]
                for at, n, sc in ((0, 256, 0), (256, 128, 384), (384, 128, 0), (512, 256, 256)):
                    ins = dve.tensor_tensor(w[:, at:at + n], s[:, sc:sc + n], x[:, at:at + n], ALU.mult)
                ins.then_inc(s_p, 1)

            def head_out(hb):
                b, h = divmod(hb, NH)
                dve.wait_ge(s_av, hb + 1)
                if hb == 0:
                    dve.wait_ge(s_em, 1)
                d, den_rt = (a.rearrange("p (r t) -> p r t", r=2) for a in (ps[:, 4:8, HD], den[:, :]))
                do(dve.scalar_tensor_tensor(out=den_rt, in0=d, scalar=-1.0,
                                            in1=exp_neg_m[:, :, 2 * b:2 * b + 2, h], op0=ALU.mult, op1=ALU.max))
                do(dve.tensor_tensor(den_rt, d, den_rt, ALU.max))
                dve.reciprocal(den_rec[:, hb, :], den[:, :]).then_inc(s_rec, 1)
                dve.wait_ge(s_rec, hb + 1)
                out = [qT[:, 2 * h + it, b * S:(b + 1) * S] for it in range(2)]
                for it in range(2):
                    dve.wait_ge(s_fwd, 2 * hb + it + 1)
                    ins = dve.scalar_tensor_tensor(out=out[it], in0=ps[:, 6 + it, 0:HD],
                                                   scalar=den_rec[:, hb, 2 + it:3 + it], in1=out[it],
                                                   op0=ALU.mult, op1=ALU.add)
                    if it == 0:
                        step_done(ins)
                ins.then_inc(s_hb, 1)
                step_done.wait()
                step_done(dve.bn_stats(head_stats[:, hb, 0, :], out[0]))
                dve.wait_ge(s_hb, hb + 1)
                do(dve.bn_stats(head_stats[:, hb, 1, :], out[1]))
                step_done(dve.bn_aggr(head_mv[:, hb, 0, :], head_stats[:, hb, 0, :]))
                dve.bn_aggr(head_mv[:, hb, 1, :], head_stats[:, hb, 1, :]).then_inc(s_hh, 1)

            def request_out(b):
                dve.wait_ge(s_hstd, b + 1)
                do(dve.reciprocal(head_rstd[:, 4 * b:4 * b + 4, :], head_std[:, 4 * b:4 * b + 4, :]))
                for it in range(2):
                    t = 2 * b + it
                    for h in range(NH):
                        part = qT[:, 2 * h + it, b * S:(b + 1) * S]
                        step_done(dve.tensor_scalar(part, part, head_mv[:, 4 * b + h, it, 0:1],
                                                    head_rstd[:, 4 * b + h, it:it + 1], ALU.subtract, ALU.mult))
                    step_done.wait()
                    dve.wait_ge(s_og, t + 1)
                    o = o_sig[:, t, :].rearrange("p (h d) -> p h d", h=NH)
                    dve.tensor_tensor(o, o, qT[:, it:8:2, b * S:(b + 1) * S], ALU.mult).then_inc(s_y, 1)

            dve.wait_ge(s_const, 2)
            head_exponents(0)
            head_exponents(1)
            for hb in range(8):
                head_weights(hb)
                if hb:
                    head_out(hb - 1)
                if hb < 6:
                    head_exponents(hb + 2)
            request_out(0)
            head_out(7)
            request_out(1)
            for t in range(NT):
                half_lo(1, t)
            for n in (18, 19):
                unit_lo(n, n % RING1, n % 2)

            def mixer_sum(call, group, unit):
                def f(t):
                    wait_bank(dve, group, unit, t)
                    if call == 0:
                        dve.wait_ge(s_res[t], 16)
                    for half in range(2):
                        zt = z[:, t, half * CG:(half + 1) * CG]
                        step_done(dve.scalar_tensor_tensor(out=zt, in0=zt, scalar=ALPHA, in1=ps[:, 4 * half + t, :],
                                                           op0=ALU.mult, op1=ALU.add))
                    step_done.wait()
                return f

            def expert_sum(call):
                def f(t):
                    n = NT * (call // 2) + t
                    dve.wait_ge(s_ax, n + 1)
                    if t < 2:
                        dve.wait_ge(s_yb[t][0], 16 * (call // 2 + 1))
                        do(dve.scalar_tensor_tensor(out=x_back[:, t, :], in0=y_back[t][:, 0, :],
                                                    scalar=gate_of[:, t, 0:1], in1=x_back[:, t, :],
                                                    op0=ALU.mult, op1=ALU.add))
                    else:
                        dve.wait_ge(s_yx, 2 * (call // 2) + t - 1)
                    dve.wait_ge(s_yb[t][1], 16 * (call // 2 + 1))
                    do(dve.scalar_tensor_tensor(out=z[:, t, :], in0=y_back[t][:, 1, :], scalar=gate_of[:, t, 1:2],
                                                in1=x_back[:, t, :], op0=ALU.mult, op1=ALU.add))
                return f

            def first_where(out, mask, order):
                do(dve.tensor_tensor(r_b_view(out), mask, order, ALU.mult))
                do(dve.tensor_reduce(r_one[:, :], r_b_view(out), AX.X, ALU.max))
                do(dve.tensor_tensor(out, r_b_view(out), r_one[:, :].unsqueeze(2).to_broadcast(list(out.shape)),
                                     ALU.is_equal))

            def r_b_view(out):
                return r_b[:, :, 0:out.shape[2]]

            def choose(layer):
                wide = lambda a, n: a.unsqueeze(2).to_broadcast([P, NT, n])
                unit_lo(SPLIT0[layer], 0, 0)
                dve.wait_ge(s_lg, layer + 1)
                dve.tensor_scalar(logits_T, ps[0:E, 0, :], rout_b[:, :], None, ALU.add).then_inc(s_lb, 1)
                dve.wait_ge(s_lt, layer + 1)
                logits = ps[:, 2, 0:NT * E].rearrange("p (t e) -> p t e", t=NT)
                do(dve.tensor_reduce(r_one[:, :], logits, AX.X, ALU.max))
                dve.tensor_tensor(r_log[:, :, :], logits, wide(r_one[:, :], E), ALU.subtract
                                  ).then_inc(s_rlog, NT)
                dve.wait_ge(s_rexp, NT * (layer + 1))
                do(dve.reciprocal(r_one[:, :], r_sum[:, :]))
                do(dve.tensor_tensor(r_prob[:, :, :], r_prob[:, :, :], wide(r_one[:, :], E), ALU.mult))
                g = r_prob[:, :, :].rearrange("p t (g e) -> p (t g) e", g=NG)
                step_done(dve.tensor_tensor(r_pair[:, :, 0:3], g[:, :, 0:3], g[:, :, 1:4], ALU.add))
                step_done(dve.tensor_tensor(r_pair[:, :, 3:5], g[:, :, 0:2], g[:, :, 2:4], ALU.add))
                do(dve.tensor_tensor(r_pair[:, :, 5:6], g[:, :, 0:1], g[:, :, 3:4], ALU.add))
                do(dve.tensor_reduce(r_score[:, :, :].rearrange("p t g -> p (t g)"), r_pair[:, :, :], AX.X, ALU.max))
                do(dve.tensor_reduce(r_one[:, :], r_score[:, :, :], AX.X, ALU.max))
                do(dve.tensor_tensor(r_group[:, :, :], r_score[:, :, :], wide(r_one[:, :], NG), ALU.is_equal))
                first_where(r_group[:, :, :], r_group[:, :, :],
                            group_first[:, :].unsqueeze(1).to_broadcast([P, NT, NG]))
                in_group = r_group[:, :, :].rearrange("p t g -> p (t g)").unsqueeze(2).to_broadcast([P, NT * NG, GE])
                grouped = lambda a: a[:, :, :].rearrange("p t (g e) -> p (t g) e", g=NG)
                do(dve.tensor_tensor(grouped(r_a), grouped(r_prob), in_group, ALU.mult))
                do(dve.tensor_scalar(grouped(r_log), in_group, -1.0, None, ALU.add))
                do(dve.tensor_tensor(r_a[:, :, :], r_a[:, :, :], r_log[:, :, :], ALU.add))
                order = expert_first[:, :].unsqueeze(1).to_broadcast([P, NT, E])
                do(dve.tensor_reduce(r_v1[:, :], r_a[:, :, :], AX.X, ALU.max))
                do(dve.tensor_tensor(is_top1[:, :, :], r_a[:, :, :], wide(r_v1[:, :], E), ALU.is_equal))
                first_where(is_top1[:, :, :], is_top1[:, :, :], order)
                do(dve.scalar_tensor_tensor(out=r_a[:, :, :], in0=is_top1[:, :, :], scalar=-4.0, in1=r_a[:, :, :],
                                            op0=ALU.mult, op1=ALU.add))
                do(dve.tensor_reduce(r_v2[:, :], r_a[:, :, :], AX.X, ALU.max))
                do(dve.tensor_tensor(is_top2[:, :, :], r_a[:, :, :], wide(r_v2[:, :], E), ALU.is_equal))
                first_where(is_top2[:, :, :], is_top2[:, :, :], order)
                dve.tensor_tensor(chosen, is_top1[:, :, :], is_top2[:, :, :], ALU.add).then_inc(s_chosen, 1)
                dve.wait_ge(s_chosen, layer + 1)
                do(dve.tensor_tensor(r_one[:, :], r_v1[:, :], r_v2[:, :], ALU.add))
                do(dve.reciprocal(r_sum[:, :], r_one[:, :]))
                do(dve.tensor_tensor(gate_of[:, :, 0], r_v1[:, :], r_sum[:, :], ALU.mult))
                do(dve.tensor_tensor(gate_of[:, :, 1], r_v2[:, :], r_sum[:, :], ALU.mult))
                do(dve.tensor_copy(values[:, :, :, 0], wide(token_no[:, :], E)))
                do(dve.scalar_tensor_tensor(out=values[:, :, :, 1], in0=is_top2[:, :, :], scalar=float(T),
                                            in1=wide(token_no[:, :], E), op0=ALU.mult, op1=ALU.add))
                dve.wait_ge(s_rank, layer + 1)
                rank = ps[:, 1, 0:NT * E].rearrange("p (t e) -> p t e", t=NT)
                do(dve.scalar_tensor_tensor(out=place[:, :, :], in0=rank, scalar=1.0, in1=chosen, op0=ALU.add,
                                            op1=ALU.mult))

            def most_of_all(layer):
                do(dve.tensor_reduce(r_max[:, :], ps[:, 1, NT * E:(NT + 1) * E], AX.X, ALU.max))
                dve.tensor_copy(most[:, :], r_max[:, :]).then_inc(s_routed, 1)

            def at_expert(a, t, e):
                return a[:, t, e:e + 1] if isinstance(e, int) else a[:, t, bass.ds(e, 1)]

            def experts(layer):
                c0 = E * layer

                def one_hots(e, j):
                    if not isinstance(e, int) or e >= 2:
                        dve.wait_ge(s_ixm, e + (c0 - 1))
                    for t in range(NT):
                        ins = dve.tensor_scalar(one_hot[:, j % 2, t, 0:P], place_no[:, :], at_expert(place, t, e), None,
                                                ALU.is_equal)
                    ins.then_inc(s_oh, 1)

                def row_numbers(e, j):
                    dve.wait_ge(s_ixm, e + (c0 + 1))
                    dst = rows_of[:, e, :] if isinstance(e, int) else \
                        rows_of[:, bass.ds(e, 1), :].rearrange("p o n -> p (o n)")
                    dve.tensor_scalar(dst, ps[:, 7, 0:2], NO_ROW, None, ALU.add).then_inc(s_ix, 1)

                def gathered_lo(e, j):
                    dve.wait_ge(s_ghi, e + (c0 + 1))
                    dst = slice((j % 2) * P, (j % 2 + 1) * P)
                    dve.tensor_tensor(xt_lo[:, :, dst], ps[:, 0:2, :].rearrange("p b (c s) -> p (b c) s", c=4),
                                      xt_hi[:, :, dst].bitcast(F32), ALU.subtract).then_inc(s_glo, 1)

                def hidden(e, j):
                    dve.wait_ge(s_silu, e + (c0 + 1))
                    if not isinstance(e, int) or e >= 2:
                        dve.wait_ge(s_htr, e + (c0 - 1))
                    dve.tensor_tensor(h_tok[:, j % 2, :], ps[:, 2 + j % 2, FE:2 * FE], silu_g[:, j % 2, :], ALU.mult
                                      ).then_inc(s_h, 1)

                def units(e, j, kh):
                    unit_lo(e * 2 + (SPLIT0[layer] + kh), 3 * j + kh, kh)

                def step(e, j, left):
                    if left > 2:
                        gathered_lo(e + 2, (j + 2) % 4)
                    if left > 4:
                        one_hots(e + 4, j)
                    if left > 2:
                        units(e + 2, (j + 2) % 4, 0)
                    if left > 1:
                        hidden(e + 1, (j + 1) % 4)
                    if left > 4:
                        row_numbers(e + 4, j)
                    if left > 2:
                        units(e + 2, (j + 2) % 4, 1)

                one_hots(0, 0)
                one_hots(1, 1)
                row_numbers(0, 0)
                most_of_all(layer)
                row_numbers(1, 1)
                one_hots(2, 2)
                units(0, 0, 1)
                row_numbers(2, 2)
                one_hots(3, 3)
                gathered_lo(0, 0)
                row_numbers(3, 3)
                gathered_lo(1, 1)
                units(1, 1, 0)
                hidden(0, 0)
                units(1, 1, 1)
                for j in range(4):
                    step(j, j, 9)
                with dve.Fori(1, 3) as turn:
                    for j in range(4):
                        step(turn * 4 + j, j, 9)
                for j in range(4):
                    step(12 + j, j, 4 - j)

            def late_experts(layer):
                L = late[layer]
                n = dve.value_load(most[0:1, 0:1], min_val=0, max_val=T)
                with dve.If(n > PLACES):
                    dve.wait_ge(s_ye, E * layer + E)
                    dve.wait_ge(s_sca[0], 16 * (E // 2) * (layer + 1))
                    dve.wait_ge(s_sca[1], 16 * (E // 2) * (layer + 1))
                    with dve.Fori(0, E) as e:
                        for r in range(1, ROUNDS):
                            n = e * (ROUNDS - 1) + r
                            for t in range(NT):
                                ins = dve.tensor_scalar(one_hot[:, 0, t, :], place_no[:, :], float(r * PLACES),
                                                        at_expert(place, t, e), ALU.add, ALU.is_equal)
                            ins.then_inc(L["oh"], 1)
                            dve.wait_ge(L["ixm"], n)
                            dve.tensor_scalar(rows_of[:, 0, :], ps[:, 7, 0:2], NO_ROW, None, ALU.add
                                              ).then_inc(L["ix"], 1)
                            dve.wait_ge(L["silu"], n)
                            dve.tensor_tensor(h_tok[:, 0, :], ps[:, 2, FE:2 * FE], silu_g[:, 0, :], ALU.mult
                                              ).then_inc(L["h"], 1)
                            dve.wait_ge(L["sca"], n * 16)

            norm(0, 2, mixer_sum(0, 9, 19))
            choose(0)
            experts(0)
            late_experts(0)
            norm(1, 3, expert_sum(1))
            dve.wait_ge(s_cwt, 1)
            dve.tensor_copy(taps[:, :, :].rearrange("p w c -> p (w c)"), ps[:, 7, 0:3 * KC]).then_inc(s_taps, 1)
            dve.wait_ge(s_taps, 1)
            unit_lo(SPLIT_CONV, 0, 0)
            per_half = 4 * 3
            with dve.Fori(0, 2) as half:
                step_done.loop(half, per_half)
                unit_lo(half * 6 + (SPLIT_CONV + 1), 1, 1)
                for g in range(3):
                    for kh in range(2):
                        if g < 2 or kh == 0:
                            u = 2 * g + kh + 2
                            unit_lo(half * 6 + (SPLIT_CONV + u), u % RING2, kh)
                    for c in range(4):
                        if g == 1:
                            wait_bank(dve, half * 3 + 11, half * 6 + (SPLIT_CONV + 3), c)
                            dve.wait_ge(s_cev, half * 4 + (c + 1))
                            dve.tensor_tensor(u_T[:, c, :], ps[:, 4 + c, :], c_T[:, c, :], ALU.mult
                                              ).then_inc(s_hev, 1)
                        elif g == 2:
                            wait_bank(dve, half * 3 + 12, half * 6 + (SPLIT_CONV + 5), c)
                            dst = g_T[:, bass.ds(half * 4 + c, 1), :].rearrange("p o t -> p (o t)")
                            dve.tensor_tensor(dst, ps[:, c, :], conv_T[:, c, :], ALU.mult).then_inc(s_hev, 1)
                    if g == 1:
                        dve.wait_ge(s_hev, half * 8 + 8)
                        for c in range(4):
                            tap = lambda w: taps[:, w, bass.ds(half * 4 + c, 1)]
                            u2 = u_T[:, c, :].rearrange("p (b t) -> p b t", b=2)
                            o2 = conv_T[:, c, :].rearrange("p (b t) -> p b t", b=2)
                            do(dve.tensor_scalar(o2, u2, tap(1), None, ALU.mult))
                            do(dve.scalar_tensor_tensor(out=o2[:, :, 1:S], in0=u2[:, :, 0:S - 1], scalar=tap(0),
                                                        in1=o2[:, :, 1:S], op0=ALU.mult, op1=ALU.add))
                            do(dve.scalar_tensor_tensor(out=o2[:, :, 0:S - 1], in0=u2[:, :, 1:S], scalar=tap(2),
                                                        in1=o2[:, :, 0:S - 1], op0=ALU.mult, op1=ALU.add))
                    if g == 2:
                        dve.wait_ge(s_hev, half * 8 + 12)
                        dve.engine_nop().then_inc(s_conv, 4)
                step_done.end(2)
            for c in range(KC):
                dve.wait_ge(s_ghx, c + 1)
                dve.tensor_tensor(xt_lo[:, c, :], g_T[:, c, :], xt_hi[:, c, :].bitcast(F32), ALU.subtract
                                  ).then_inc(s_glx, 1)
            for n in (13, 14, 15):
                unit_lo(SPLIT_CONV + n, n % RING2, n % 2)
            norm(2, 4, mixer_sum(2, 17, SPLIT_CONV + 15))
            choose(1)
            experts(1)
            late_experts(1)
            norm(3, 0, expert_sum(3))

        @block.gpsimd
        def _(pool):
            done = Steps(pool, s_pool)
            last_token, last_result = pool.to_reg(T - 1), pool.to_reg(2 * T - 1)
            x_tiles = [x_prompt[0, 0:P, :], x_prompt[0, P:S, :], x_sample[0, 0:P, :], x_sample[0, P:S, :]]

            def spread(row):
                return row.rearrange("(o n) -> o n", o=1).to_broadcast([P, D])

            done(pool.memset(ident[:, :], 0.0))
            done.wait()
            pool.affine_select(out=ident[:, :], in_=ident[:, :], compare_op=ALU.not_equal, fill=1.0, base=0,
                               pattern=[[-1, P]], channel_multiplier=1).then_inc(s_const, 1)
            pool.dma_start(ln_g[:, :], spread(mlstm_norm_g[0])).then_inc(s_lnp, 16)
            done(pool.memset(pick_head[:, :, :], 0.0))
            done(pool.memset(mask_fw[:, :], 0.0))
            done(pool.memset(mask_bw[:, :], 0.0))
            done(pool.memset(earlier[:, :].bitcast(F32), 0.0))
            done(pool.memset(all_ones[:, :].bitcast(F32), 1.0))
            done(pool.memset(chosen_pad[:, :, :].bitcast(F32), 0.0))
            done(pool.memset(eps_ln[:, :], LN_EPS))
            done(pool.memset(eps_head[:, :], HEAD_EPS))
            done.wait()
            done(pool.affine_select(out=pick_head[:, :, :], in_=pick_head[:, :, :], compare_op=ALU.not_equal,
                                    fill=1.0, base=0, pattern=[[1, NH], [0, P]], channel_multiplier=-1))
            done(pool.affine_select(out=mask_fw[:, :], in_=mask_fw[:, :], compare_op=ALU.is_ge, fill=NEG,
                                    base=0, pattern=[[1, S]], channel_multiplier=-1))
            done(pool.affine_select(out=mask_bw[:, :], in_=mask_bw[:, :], compare_op=ALU.is_ge, fill=NEG,
                                    base=P, pattern=[[-1, S]], channel_multiplier=1))
            done(pool.affine_select(out=earlier[:, :], in_=earlier[:, :], compare_op=ALU.is_ge, fill=1.0,
                                    base=0, pattern=[[-1, P]], channel_multiplier=1))
            done(pool.iota(place_no[:, :], pattern=[[1, P]], base=1, channel_multiplier=0,
                           allow_small_or_imprecise_dtypes=True))
            done(pool.iota(token_no[:, :], pattern=[[P, NT]], base=-int(NO_ROW), channel_multiplier=1,
                           allow_small_or_imprecise_dtypes=True))
            done(pool.iota(group_first[:, :], pattern=[[-1, NG]], base=NG, channel_multiplier=0,
                           allow_small_or_imprecise_dtypes=True))
            done(pool.iota(expert_first[:, :], pattern=[[-1, E]], base=E, channel_multiplier=0,
                           allow_small_or_imprecise_dtypes=True))
            if PLACES < P:
                done.wait()
                done(pool.affine_select(out=place_no[:, :], in_=place_no[:, :], compare_op=ALU.is_ge, fill=1e6,
                                        base=PLACES - 1, pattern=[[-1, P]], channel_multiplier=0))
            done.wait()
            pool.engine_nop().then_inc(s_const, 1)
            pool.wait_ge(s_lnp, 16)
            pool.wait_ge(s_free, BANK_CREDIT + 32)
            for t in range(NT):
                pool.tensor_tensor(o_sig[:, t, :], o_sig[:, t, :], ln_g[:, :], ALU.mult).then_inc(s_og, 1)
            pool.wait_ge(s_og, NT)

            def norm_weights(call, g, b):
                pool.dma_start(ln_g[:, :], spread(g)).then_inc(s_lnp, 16)
                pool.dma_start(ln_b[:, :], spread(b)).then_inc(s_lnp, 16)

            def norm_end(call):
                pool.wait_ge(s_lnp, 16 + 32 * (call + 1))
                for t in range(NT - 1):
                    pool.wait_ge(s_zn, (NT - 1) * call + t + 1)
                    pool.tensor_tensor(z[:, t, :], z[:, t, :], ln_b[:, :], ALU.add).then_inc(s_xr, 1)
                for t in (NT - 2, NT - 1):
                    wait_x(pool, call, t)

            def experts(layer):
                source, target = x_dram[layer], y_dram[layer]
                pool.wait_ge(s_st_x, 64 * (layer + 1))
                pool.wait_ge(s_tr, 8 * (3 + 2 * layer))
                pool.memset(xg[:, :, :], 0.0).then_inc(s_xg0, 1)
                pool.wait_ge(s_xg0, layer + 1)
                c0 = E * layer

                def gather(e, j):
                    pool.wait_ge(s_ix, e + (c0 + 1))
                    if not isinstance(e, int) or e >= 2:
                        pool.wait_ge(s_gtr, e + (c0 - 1))
                    pool.indirect_dma_start(out=xg[:, j % 2, :], out_offset=None, in_=source,
                                            in_offset=bass.IndirectOffsetOnAxis(rows_of[:, e, 0:1], 0),
                                            bounds_check=last_token, oob_is_err=False).then_inc(s_gat[j % 2], 16)

                def scatter(e, j):
                    pool.wait_ge(s_ye, e + (c0 + 1))
                    pool.indirect_dma_start(out=target, out_offset=bass.IndirectOffsetOnAxis(rows_of[:, e, 1:2], 0),
                                            in_=ye[:, j % 2, :], in_offset=None,
                                            bounds_check=last_result, oob_is_err=False).then_inc(s_sca[j % 2], 16)

                for e in range(4):
                    gather(e, e)
                for e in range(E):
                    if e + 4 < E:
                        gather(e + 4, e % 4)
                    scatter(e, e % 4)
                for b in range(2):
                    pool.wait_ge(s_sca[b], 16 * (E // 2) * (layer + 1))

                L = late[layer]
                n = pool.value_load(most[0:1, 0:1], min_val=0, max_val=T)
                limit = pool.alloc_register()
                one_less = pool.to_reg(T - 2), pool.to_reg(2 * T - 2)
                with pool.If(n > PLACES):
                    with pool.Fori(0, E) as e:
                        for r in range(1, ROUNDS):
                            n = e * (ROUNDS - 1) + r
                            pool.wait_ge(L["ix"], n)
                            pool.reg_add(limit, one_less[0], 1)
                            pool.indirect_dma_start(out=xg[:, 0, :], out_offset=None, in_=source,
                                                    in_offset=bass.IndirectOffsetOnAxis(rows_of[:, 0, 0:1], 0),
                                                    bounds_check=limit, oob_is_err=False).then_inc(L["gat"], 16)
                            pool.wait_ge(L["ye"], n)
                            pool.reg_add(limit, one_less[1], 1)
                            pool.indirect_dma_start(out=target,
                                                    out_offset=bass.IndirectOffsetOnAxis(rows_of[:, 0, 1:2], 0),
                                                    in_=ye[:, 0, :], in_offset=None,
                                                    bounds_check=limit, oob_is_err=False).then_inc(L["sca"], 16)
                            pool.wait_ge(L["sca"], n * 16)

            def first_results(layer):
                for t in (2, 3):
                    pool.wait_ge(s_ax, NT * layer + t + 1)
                    pool.wait_ge(s_yg, 2 * layer + t - 1)
                    pool.tensor_tensor(x_back[:, t, :], x_back[:, t, :], y_back[t][:, 0, :], ALU.add
                                       ).then_inc(s_yx, 1)

            pool.wait_ge(s_e, 8)
            norm_weights(0, ln1_g[0], ln1_b[0])
            pool.wait_ge(s_mb, 8)
            for t in range(NT):
                pool.dma_start(z[:, t, :], x_tiles[t]).then_inc(s_res[t], 16)
            norm_end(0)
            norm_weights(1, ln2_g[0], ln2_b[0])
            experts(0)
            pool.dma_start(conv_rows, conv_w[0].rearrange("w (c p) -> (w c) p", p=P)).then_inc(s_cwl, 16)
            first_results(0)
            norm_end(1)
            norm_weights(2, ln1_g[1], ln1_b[1])
            norm_end(2)
            norm_weights(3, ln2_g[1], ln2_b[1])
            experts(1)
            first_results(1)
            norm_end(3)


_INS = ["x_prompt", "x_sample", "router_w", "router_b", "mlstm_w_in", "mlstm_b_gate", "mlstm_norm_g", "mlstm_w_out",
        "conv_w_in", "conv_w", "conv_w_out", "ln1_g", "ln1_b", "moe_w_gu", "moe_w_down", "ln2_g", "ln2_b"]


def kernel(**inputs):
    import numpy as np
    import concourse.bacc as bacc
    from concourse.bass_utils import run_bass_kernel_spmd

    nc = bacc.Bacc("TRN2", target_bir_lowering=False, num_devices=1)
    arrays, args = {}, []
    for name in _INS:
        a = np.ascontiguousarray(inputs[name])
        arrays[f"in_{name}"] = a
        args.append(nc.dram_tensor(f"in_{name}", a.shape, mybir.dt.from_np(a.dtype), kind="ExternalInput").ap())
    for name in ("x_prompt", "x_sample"):
        a = inputs[name]
        args.append(nc.dram_tensor(f"out_{name}", a.shape, F32, kind="ExternalOutput").ap())
    trunk(nc, *args)
    r = run_bass_kernel_spmd(nc, [arrays], core_ids=[0])
    return r.results[0]["out_x_prompt"], r.results[0]["out_x_sample"]
```
